# Optimizing a Trainium2 kernel written in Bass

```python
import math
import jax
import jax.numpy as jnp
from jax import lax
import numpy as np

D_MODEL = 2048
BATCH = 1
SEQ = 256
DEPTH = 2

N_EVEN = (DEPTH + 1) // 2
N_ODD = DEPTH // 2
NORM_EPS = 1e-6

SSM_INNER = D_MODEL
SSM_HEADDIM = 64
SSM_HEADS = SSM_INNER // SSM_HEADDIM
SSM_GROUPS = 4
SSM_HEADS_PER_GROUP = SSM_HEADS // SSM_GROUPS
SSM_STATE = 128
SSM_CONV_WIDTH = 4
SSM_CHUNK = 128
SSM_CONV_DIM = SSM_INNER + 2 * SSM_GROUPS * SSM_STATE
CONF_WIDTH = D_MODEL // 2
CONF_CONV_WIDTH = 31
AB_IN = SSM_INNER + SSM_CONV_DIM + SSM_HEADS + 2 * CONF_WIDTH
AB_OUT = SSM_INNER + CONF_WIDTH
SC_WIDTH = D_MODEL // 2
SC_CONV_WIDTH = 3
NSA_HEAD_DIM = 128
NSA_HEADS = D_MODEL // NSA_HEAD_DIM
NSA_KV_HEADS = 4
NSA_GROUP = NSA_HEADS // NSA_KV_HEADS
CMP_BLOCK = 32
CMP_STRIDE = 16
SLC_BLOCK = 64
N_SELECT = 16
N_LOCAL = 2
WINDOW = 512
NSA_QBLOCK = 32
ROPE_THETA = 10000.0
NSA_Q = NSA_HEADS * NSA_HEAD_DIM
NSA_KV = NSA_KV_HEADS * NSA_HEAD_DIM
CD_IN = 3 * SC_WIDTH + NSA_Q + 6 * NSA_KV + 3 * NSA_HEADS
CD_OUT = SC_WIDTH + NSA_Q
D_FF = 256 * ((8 * D_MODEL // 3 + 255) // 256)
FFN_CONV_WIDTH = 3
NEG_BIG = -1e30
FORCE = 1e9

kernel_name = "hybrid_ssd_conformer_shortconv_nsa_trunk"

def split_cols(x, sizes):
    return jnp.split(x, [int(c) for c in np.cumsum(sizes)[:-1]], axis=-1)

def rmsnorm(x, g):
    xf = x.astype(jnp.float32)
    y = xf * lax.rsqrt(jnp.mean(xf * xf, axis=-1, keepdims=True) + NORM_EPS)
    return (y * g.astype(jnp.float32)).astype(x.dtype)

def layernorm(x, g, b):
    xf = x.astype(jnp.float32)
    mu = jnp.mean(xf, axis=-1, keepdims=True)
    var = jnp.mean(jnp.square(xf - mu), axis=-1, keepdims=True)
    y = (xf - mu) * lax.rsqrt(var + NORM_EPS) * g.astype(jnp.float32) + b.astype(jnp.float32)
    return y.astype(x.dtype)

def causal_dwconv(x, w, b=None):
    width, ch = w.shape
    y = lax.conv_general_dilated(
        x, w[:, None, :].astype(x.dtype), window_strides=(1,), padding=[(width - 1, 0)],
        dimension_numbers=("NWC", "WIO", "NWC"), feature_group_count=ch)
    return y if b is None else y + b

def rope(x, pos):
    half = x.shape[-1] // 2
    inv = ROPE_THETA ** (-jnp.arange(half, dtype=jnp.float32) / half)
    ang = pos.astype(jnp.float32)[..., None] * inv
    cos = jnp.cos(ang)[:, :, None, :]
    sin = jnp.sin(ang)[:, :, None, :]
    xf = x.astype(jnp.float32)
    x1, x2 = xf[..., :half], xf[..., half:]
    return jnp.concatenate([x1 * cos - x2 * sin, x2 * cos + x1 * sin], axis=-1).astype(x.dtype)

def masked_softmax(s, mask):
    s = jnp.where(mask, s.astype(jnp.float32), NEG_BIG)
    return jax.nn.softmax(s, axis=-1) * mask

def ssd_chunked(xh, dt, a, bmat, cmat):
    bsz, seq = xh.shape[:2]
    nc = seq // SSM_CHUNK
    x = (xh * dt[..., None]).reshape(bsz, nc, SSM_CHUNK, SSM_GROUPS, SSM_HEADS_PER_GROUP, SSM_HEADDIM)
    la = jnp.moveaxis((dt * a).reshape(bsz, nc, SSM_CHUNK, SSM_GROUPS, SSM_HEADS_PER_GROUP), 2, -1)
    cum = jnp.cumsum(la, axis=-1)
    bm = bmat.reshape(bsz, nc, SSM_CHUNK, SSM_GROUPS, SSM_STATE)
    cm = cmat.reshape(bsz, nc, SSM_CHUNK, SSM_GROUPS, SSM_STATE)
    causal = jnp.tril(jnp.ones((SSM_CHUNK, SSM_CHUNK), dtype=bool))
    decay = jnp.exp(jnp.where(causal, cum[..., :, None] - cum[..., None, :], -jnp.inf))
    cb = jnp.einsum("bclgn,bcsgn->bcgls", cm, bm)
    y_diag = jnp.einsum("bcgls,bcgels,bcsgep->bclgep", cb, decay, x)
    decay_to_end = jnp.exp(cum[..., -1:] - cum)
    states = jnp.einsum("bcsgn,bcges,bcsgep->bcgepn", bm, decay_to_end, x)
    chunk_decay = jnp.exp(cum[..., -1])

    def step(h, inp):
        d_c, st_c = inp
        return h * d_c[..., None, None] + st_c, h

    h0 = jnp.zeros((bsz, SSM_GROUPS, SSM_HEADS_PER_GROUP, SSM_HEADDIM, SSM_STATE), jnp.float32)
    _, h_in = lax.scan(step, h0, (jnp.moveaxis(chunk_decay, 1, 0), jnp.moveaxis(states, 1, 0)))
    h_in = jnp.moveaxis(h_in, 0, 1)
    y_off = jnp.einsum("bclgn,bcgepn,bcgel->bclgep", cm, h_in, jnp.exp(cum))
    return (y_diag + y_off).reshape(bsz, seq, SSM_GROUPS, SSM_HEADS_PER_GROUP, SSM_HEADDIM)

def even_mixer(h, w_in, conv_w, conv_b, dt_bias, a_log, d_skip, ssm_norm,
               conf_dw_w, conf_dw_b, conf_ln_g, conf_ln_b, w_out):
    bsz, seq, _ = h.shape
    f32 = jnp.float32
    proj = h @ w_in
    z, xbc, dt_raw, glu = split_cols(proj, [SSM_INNER, SSM_CONV_DIM, SSM_HEADS, 2 * CONF_WIDTH])
    xbc = jax.nn.silu(causal_dwconv(xbc, conv_w, conv_b))
    xs, bm, cm = split_cols(xbc, [SSM_INNER, SSM_GROUPS * SSM_STATE, SSM_GROUPS * SSM_STATE])
    dt = jax.nn.softplus(dt_raw.astype(f32) + dt_bias.astype(f32))
    dt = dt.reshape(bsz, seq, SSM_GROUPS, SSM_HEADS_PER_GROUP)
    a = -jnp.exp(a_log.astype(f32)).reshape(SSM_GROUPS, SSM_HEADS_PER_GROUP)
    xh = xs.astype(f32).reshape(bsz, seq, SSM_GROUPS, SSM_HEADS_PER_GROUP, SSM_HEADDIM)
    y = ssd_chunked(xh, dt, a,
                    bm.astype(f32).reshape(bsz, seq, SSM_GROUPS, SSM_STATE),
                    cm.astype(f32).reshape(bsz, seq, SSM_GROUPS, SSM_STATE))
    y = y + d_skip.astype(f32).reshape(SSM_GROUPS, SSM_HEADS_PER_GROUP)[..., None] * xh
    y = y.reshape(bsz, seq, SSM_INNER).astype(h.dtype) * jax.nn.silu(z)
    y = rmsnorm(y.reshape(bsz, seq, SSM_GROUPS, -1), ssm_norm.reshape(SSM_GROUPS, -1)).reshape(bsz, seq, SSM_INNER)
    ua, ug = jnp.split(glu, 2, axis=-1)
    u = ua * jax.nn.sigmoid(ug)
    u = causal_dwconv(u, conf_dw_w, conf_dw_b)
    u = jax.nn.silu(layernorm(u, conf_ln_g, conf_ln_b))
    return jnp.concatenate([y, u], axis=-1) @ w_out

def nsa_attention(q, k_cmp_tok, v_cmp_tok, k_slc, v_slc, k_win, v_win, gates, positions,
                  cmp_pe, cmp_w1, cmp_w2):
    bsz, seq = q.shape[:2]
    dt = q.dtype
    scale = NSA_HEAD_DIM ** -0.5
    q = rope(q, positions)
    k_slc = rope(k_slc, positions)
    k_win = rope(k_win, positions)
    qg = q.reshape(bsz, seq, NSA_KV_HEADS, NSA_GROUP, NSA_HEAD_DIM)
    t = jnp.arange(seq)

    n_cmp = (seq - CMP_BLOCK) // CMP_STRIDE + 1
    starts = jnp.arange(n_cmp) * CMP_STRIDE
    ends = starts + CMP_BLOCK - 1
    idx = starts[:, None] + jnp.arange(CMP_BLOCK)[None, :]

    def compress(tok, pe, w1, w2):
        blk = tok[:, idx] + pe[:, None, :]
        blk = jnp.moveaxis(blk, 3, 2).reshape(bsz, n_cmp, NSA_KV_HEADS, CMP_BLOCK * NSA_HEAD_DIM)
        return jax.nn.silu(blk @ w1) @ w2

    kc = rope(compress(k_cmp_tok, cmp_pe[0], cmp_w1[0], cmp_w2[0]), positions[:, ends])
    vc = compress(v_cmp_tok, cmp_pe[1], cmp_w1[1], cmp_w2[1])
    s_cmp = jnp.einsum("bsged,bngd->bsgen", qg, kc) * scale
    cmp_mask = (ends[None, :] <= t[:, None])[None, :, None, None, :]
    p_cmp = masked_softmax(s_cmp, cmp_mask)
    o_cmp = jnp.einsum("bsgen,bngd->bsged", p_cmp.astype(dt), vc)

    n_slc = seq // SLC_BLOCK
    n_sel = min(N_SELECT, n_slc)
    j = jnp.arange(n_slc)
    overlap = ((starts[:, None] < (j[None, :] + 1) * SLC_BLOCK)
               & (ends[:, None] >= j[None, :] * SLC_BLOCK)).astype(jnp.float32)
    imp = jnp.einsum("bsgen,nj->bsgj", p_cmp, overlap)
    cur = (t // SLC_BLOCK)[:, None]
    forced = (j[None, :] == 0) | ((j[None, :] <= cur) & (j[None, :] > cur - N_LOCAL))
    valid = j[None, :] * SLC_BLOCK <= t[:, None]
    imp = jnp.where(forced[None, :, None, :], FORCE, jnp.where(valid[None, :, None, :], imp, -FORCE))
    _, sel = lax.top_k(imp, n_sel)

    kb = jnp.moveaxis(k_slc.reshape(bsz, n_slc, SLC_BLOCK, NSA_KV_HEADS, NSA_HEAD_DIM), 3, 1)
    vb = jnp.moveaxis(v_slc.reshape(bsz, n_slc, SLC_BLOCK, NSA_KV_HEADS, NSA_HEAD_DIM), 3, 1)
    kpad = jnp.pad(k_win, ((0, 0), (WINDOW, 0), (0, 0), (0, 0)))
    vpad = jnp.pad(v_win, ((0, 0), (WINDOW, 0), (0, 0), (0, 0)))
    bi = jnp.arange(bsz)[:, None, None, None]
    gi = jnp.arange(NSA_KV_HEADS)[None, None, :, None]
    n_qb = seq // NSA_QBLOCK
    band = WINDOW + NSA_QBLOCK

    def query_block(args):
        qb, selb, i = args
        tq = i * NSA_QBLOCK + jnp.arange(NSA_QBLOCK)
        ks = kb[bi, gi, selb]
        vs = vb[bi, gi, selb]
        s = jnp.einsum("bqged,bqgnld->bqgenl", qb, ks) * scale
        kpos = selb[..., None] * SLC_BLOCK + jnp.arange(SLC_BLOCK)
        m = (kpos <= tq[None, :, None, None, None])[:, :, :, None]
        p = masked_softmax(s.reshape(s.shape[:4] + (-1,)), m.reshape(m.shape[:4] + (-1,)))
        o_s = jnp.einsum("bqgek,bqgkd->bqged", p.astype(dt),
                         vs.reshape(bsz, NSA_QBLOCK, NSA_KV_HEADS, -1, NSA_HEAD_DIM))
        kw = lax.dynamic_slice_in_dim(kpad, i * NSA_QBLOCK, band, axis=1)
        vw = lax.dynamic_slice_in_dim(vpad, i * NSA_QBLOCK, band, axis=1)
        s = jnp.einsum("bqged,bkgd->bqgek", qb, kw) * scale
        kp = i * NSA_QBLOCK - WINDOW + jnp.arange(band)
        mw = (kp[None, :] <= tq[:, None]) & (kp[None, :] > tq[:, None] - WINDOW) & (kp[None, :] >= 0)
        p = masked_softmax(s, mw[None, :, None, None, :])
        o_w = jnp.einsum("bqgek,bkgd->bqged", p.astype(dt), vw)
        return o_s, o_w

    qblk = jnp.moveaxis(qg.reshape(bsz, n_qb, NSA_QBLOCK, NSA_KV_HEADS, NSA_GROUP, NSA_HEAD_DIM), 1, 0)
    sblk = jnp.moveaxis(sel.reshape(bsz, n_qb, NSA_QBLOCK, NSA_KV_HEADS, n_sel), 1, 0)
    o_slc, o_win = lax.map(query_block, (qblk, sblk, jnp.arange(n_qb)))
    shp = (bsz, seq, NSA_KV_HEADS, NSA_GROUP, NSA_HEAD_DIM)
    o_slc = jnp.moveaxis(o_slc, 0, 1).reshape(shp)
    o_win = jnp.moveaxis(o_win, 0, 1).reshape(shp)
    g = jax.nn.sigmoid(gates.astype(jnp.float32)).astype(dt).reshape(bsz, seq, NSA_KV_HEADS, NSA_GROUP, 3)
    o = g[..., 0:1] * o_cmp + g[..., 1:2] * o_slc + g[..., 2:3] * o_win
    return o.reshape(bsz, seq, NSA_Q)

def odd_mixer(h, positions, w_in, sc_conv_w, cmp_pe, cmp_w1, cmp_w2, w_out):
    bsz, seq, _ = h.shape
    proj = h @ w_in
    sc_b, sc_c, sc_h, q, kc, vc, ks, vs, kw, vw, gates = split_cols(
        proj, [SC_WIDTH] * 3 + [NSA_Q] + [NSA_KV] * 6 + [3 * NSA_HEADS])
    y_c = sc_b * causal_dwconv(sc_c * sc_h, sc_conv_w)
    kv = lambda a: a.reshape(bsz, seq, NSA_KV_HEADS, NSA_HEAD_DIM)
    y_d = nsa_attention(q.reshape(bsz, seq, NSA_HEADS, NSA_HEAD_DIM), kv(kc), kv(vc), kv(ks), kv(vs),
                        kv(kw), kv(vw), gates, positions, cmp_pe, cmp_w1, cmp_w2)
    return jnp.concatenate([y_c, y_d], axis=-1) @ w_out

def conv_ffn(h, w_up, conv_w, conv_b, w_down):
    u = causal_dwconv(h @ w_up, conv_w, conv_b)
    g, v = jnp.split(u, 2, axis=-1)
    return (jax.nn.silu(g) * v) @ w_down

def setup_inputs(seed: int = 0) -> dict:
    key = jax.random.key(seed)
    keys = iter(jax.random.split(key, 40))

    def normal(shape, scale):
        return scale * jax.random.normal(next(keys), shape, jnp.float32)

    def gain(shape):
        return 1.0 + normal(shape, 0.02)

    out_scale = (2.0 * DEPTH) ** -0.5
    x = jax.random.normal(next(keys), (BATCH, SEQ, D_MODEL), jnp.float32)
    offset = jax.random.randint(next(keys), (BATCH, 1), 0, 1024, dtype=jnp.int32)
    positions = offset + jnp.arange(SEQ, dtype=jnp.int32)[None, :]
    dt0 = jnp.exp(jax.random.uniform(next(keys), (N_EVEN, SSM_HEADS), jnp.float32,
                                     math.log(1e-3), math.log(1e-1)))
    ssm_dt_bias = dt0 + jnp.log(-jnp.expm1(-dt0))
    ssm_a_log = jnp.log(jax.random.uniform(next(keys), (N_EVEN, SSM_HEADS), jnp.float32, 1.0, 16.0))
    return {
        "x": x,
        "positions": positions,
        "mix_norm": gain((DEPTH, D_MODEL)),
        "ffn_norm": gain((DEPTH, D_MODEL)),
        "final_norm": gain((D_MODEL,)),
        "ab_w_in": normal((N_EVEN, D_MODEL, AB_IN), D_MODEL ** -0.5),
        "ssm_conv_w": normal((N_EVEN, SSM_CONV_WIDTH, SSM_CONV_DIM), SSM_CONV_WIDTH ** -0.5),
        "ssm_conv_b": normal((N_EVEN, SSM_CONV_DIM), 0.01),
        "ssm_dt_bias": ssm_dt_bias,
        "ssm_a_log": ssm_a_log,
        "ssm_d": gain((N_EVEN, SSM_HEADS)),
        "ssm_norm": gain((N_EVEN, SSM_INNER)),
        "conf_dw_w": normal((N_EVEN, CONF_CONV_WIDTH, CONF_WIDTH), CONF_CONV_WIDTH ** -0.5),
        "conf_dw_b": normal((N_EVEN, CONF_WIDTH), 0.01),
        "conf_ln_g": gain((N_EVEN, CONF_WIDTH)),
        "conf_ln_b": normal((N_EVEN, CONF_WIDTH), 0.01),
        "ab_w_out": normal((N_EVEN, AB_OUT, D_MODEL), AB_OUT ** -0.5 * out_scale),
        "cd_w_in": normal((N_ODD, D_MODEL, CD_IN), D_MODEL ** -0.5),
        "sc_conv_w": normal((N_ODD, SC_CONV_WIDTH, SC_WIDTH), SC_CONV_WIDTH ** -0.5),
        "nsa_cmp_pe": normal((N_ODD, 2, CMP_BLOCK, NSA_HEAD_DIM), 0.1),
        "nsa_cmp_w1": normal((N_ODD, 2, CMP_BLOCK * NSA_HEAD_DIM, NSA_HEAD_DIM), (CMP_BLOCK * NSA_HEAD_DIM) ** -0.5),
        "nsa_cmp_w2": normal((N_ODD, 2, NSA_HEAD_DIM, NSA_HEAD_DIM), NSA_HEAD_DIM ** -0.5),
        "cd_w_out": normal((N_ODD, CD_OUT, D_MODEL), CD_OUT ** -0.5 * out_scale),
        "ffn_w_up": normal((DEPTH, D_MODEL, 2 * D_FF), D_MODEL ** -0.5),
        "ffn_conv_w": normal((DEPTH, FFN_CONV_WIDTH, 2 * D_FF), FFN_CONV_WIDTH ** -0.5),
        "ffn_conv_b": normal((DEPTH, 2 * D_FF), 0.01),
        "ffn_w_down": normal((DEPTH, D_FF, D_MODEL), D_FF ** -0.5 * out_scale),
    }

def reference(x, positions, mix_norm, ffn_norm, final_norm, ab_w_in, ssm_conv_w, ssm_conv_b,
              ssm_dt_bias, ssm_a_log, ssm_d, ssm_norm, conf_dw_w, conf_dw_b, conf_ln_g, conf_ln_b,
              ab_w_out, cd_w_in, sc_conv_w, nsa_cmp_pe, nsa_cmp_w1, nsa_cmp_w2, cd_w_out,
              ffn_w_up, ffn_conv_w, ffn_conv_b, ffn_w_down):
    h = x
    for layer in range(DEPTH):
        i = layer // 2
        u = rmsnorm(h, mix_norm[layer])
        if layer % 2 == 0:
            h = h + even_mixer(u, ab_w_in[i], ssm_conv_w[i], ssm_conv_b[i], ssm_dt_bias[i], ssm_a_log[i],
                               ssm_d[i], ssm_norm[i], conf_dw_w[i], conf_dw_b[i], conf_ln_g[i],
                               conf_ln_b[i], ab_w_out[i])
        else:
            h = h + odd_mixer(u, positions, cd_w_in[i], sc_conv_w[i], nsa_cmp_pe[i], nsa_cmp_w1[i],
                              nsa_cmp_w2[i], cd_w_out[i])
        u = rmsnorm(h, ffn_norm[layer])
        h = h + conv_ffn(u, ffn_w_up[layer], ffn_conv_w[layer], ffn_conv_b[layer], ffn_w_down[layer])
    return rmsnorm(h, final_norm)


_drawn_inputs = setup_inputs


def setup_inputs(seed=0):
    import zlib

    import numpy as np

    out = dict(_drawn_inputs(seed))
    spreads = {}
    factors = {'mix_norm': 3.533,
     'ffn_norm': 4.927,
     'final_norm': 21.593,
     'ssm_conv_b': 8.0,
     'ssm_d': 200.0,
     'ssm_norm': 6.917,
     'conf_dw_b': 8.0,
     'conf_ln_g': 8.0,
     'conf_ln_b': 40.245,
     'nsa_cmp_pe': 30.391,
     'ffn_conv_b': 8.0}
    for name, (base, spread) in spreads.items():
        noise = np.random.default_rng([zlib.crc32(name.encode()), seed]).standard_normal(out[name].shape)
        drawn = base * np.exp(spread * noise) if base else spread * noise
        out[name] = jnp.asarray(drawn.astype(out[name].dtype))
    for name, factor in factors.items():
        out[name] = (out[name] * factor).astype(out[name].dtype)
    return out
```

```python
from contextlib import ExitStack

import numpy as np
import concourse.bass as bass
from concourse import mybir

F32 = mybir.dt.float32
F32R = mybir.dt.float32r
I32 = mybir.dt.int32
ACT = mybir.ActivationFunctionType
ALU = mybir.AluOpType
AXX = mybir.AxisListType.X
ds = bass.ds

P = 128
D = 2048
SEQ = 256
NT = SEQ // P
DT = D // P
EPS = 1e-6
ARENA = 53152
CW = 512
RING = 4
UNIT = 4 * CW

HEADS, GROUPS, HP, STATE = 32, 4, 64, 128
HPG = HEADS // GROUPS
SSM_TILES = D // P
CONF_TILES = 8
CONF_TAPS = 31
POOL_CONF = 3
CONV_DIM = D + 2 * GROUPS * STATE
ZC, XBCC, DTC, GLUC = 0, D, D + CONV_DIM, D + CONV_DIM + HEADS
NSA_HEADS, KVH, HD = 16, 4, 128
SC = 1024
QC, KVC, GATEC = 3 * SC, 3 * SC + D, 3 * SC + D + 6 * KVH * HD
NGATE = 3 * NSA_HEADS
CB, CSTRIDE = 32, 16
NCMP = (SEQ - CB) // CSTRIDE + 1
SCALE = float(HD) ** -0.5
NEG = -1e30
FT = 44
FF = FT * P
CHUNKS = [(0, 16), (16, 16), (32, 12)]


class Span:

    def __init__(self, unit, tile, groups, units, kt):
        self.unit, self.tile, self.groups, self.units, self.kt = unit, tile, groups, units, kt
        self.unit_end, self.tile_end = unit + groups * units, tile + 4 * groups


def mlp_conv0(layer):
    return 4 * EVEN_XBC_GROUPS + (SC // P if layer else 0)


def plan():
    spans, unit, tile = {}, 0, 0

    def add(name, groups, units, kt):
        nonlocal unit, tile
        spans[name] = Span(unit, tile, groups, units, kt)
        unit, tile = spans[name].unit_end, spans[name].tile_end

    for layer in range(2):
        add(f"in{layer}", (14, 16)[layer], 4, 4)
        add(f"out{layer}", 4, 8, 3)
        for b, (_, n) in enumerate(CHUNKS):
            add(f"up{layer}{b}", n // 2, 4, 4)
            add(f"down{layer}{b}", 4, 4, n // 4)
    return spans


SPANS = plan()


def kt_at(unit):
    return next((s.kt for s in SPANS.values() if s.unit <= unit < s.unit_end), 4)


def ahead(e, step, n, offsets=(2, 3, 4, 5)):
    kts = [kt_at(e + k) for k in offsets]
    assert all([kt_at(e + k + i * step) for k in offsets] == kts for i in range(n)), (e, step, n)
    return kts


LAST_UNIT = max(s.unit_end for s in SPANS.values())


def rest(e):
    return [kt_at(u) for u in range(e + 2, e + 6) if u < LAST_UNIT]


PLAIN = {}
_n = 0
for _name, _s in SPANS.items():
    if _name[:2] in ("in", "up"):
        PLAIN[_name] = _n
        _n += 4 * _s.groups
EVEN_XBC_GROUPS = 6
CONV = {"in0": 0}
_n = 4 * EVEN_XBC_GROUPS
for _l in range(2):
    if _l == 1:
        CONV["in1"] = _n
        _n += SC // P
    for _b, (_, _c) in enumerate(CHUNKS):
        CONV[f"up{_l}{_b}"] = _n
        _n += 2 * _c

HALVES = {}
_n = 0
for _name, _s in SPANS.items():
    if _name not in PLAIN:
        HALVES[_name] = _n
        _n += 4 * _s.groups
COMPRESS = (3, 5, 7)
CONSTS = 8
EXPS = [2 * (m + 1) + 2 * (m // 2) for m in range(2 * GROUPS)]
ROUNDER = float(1.5 * 2 ** 23)
PI = 3.1415925


def _turn_parts():
    first = 6.28125
    second = float(np.float32(np.floor((2 * np.pi - first) * 2 ** 20) / 2 ** 20))
    return first, second, float(np.float32(2 * np.pi - first - second))


TURN = _turn_parts()


PARAMS = {}
_c = 0
for _name, _r in (("mix", 32), ("ffn", 32), ("final", 16), ("sconv_w", 96), ("sconv_b", 24),
                  ("snorm", 16), ("dw_w", 248), ("dw_b", 8), ("ln_g", 8), ("ln_b", 8),
                  ("sc_w", 24), ("pe", 64), ("fconv_w", 528), ("fconv_b", 176)):
    PARAMS[_name] = (_c, _r)
    _c += _r
NPARAM = _c
PTILES = -(-NPARAM // P)
PAR_LOADS = sum((c + n - 1) // P - c // P + 1 for c, n in PARAMS.values())


def build(nc, x, positions, inv_freq, mix_norm, ffn_norm, final_norm, ab_w_in, ssm_conv_w, ssm_conv_b,
          ssm_dt_bias, ssm_a_log, ssm_d, ssm_norm, conf_dw_w, conf_dw_b, conf_ln_g, conf_ln_b,
          ab_w_out, cd_w_in, sc_conv_w, nsa_cmp_pe, nsa_cmp_w1, nsa_cmp_w2, cd_w_out,
          ffn_w_up, ffn_conv_w, ffn_conv_b, ffn_w_down, out):
    stack = ExitStack()
    with stack:
        base = (nc.sbuf_base + 31) // 32 * 32
        stack.enter_context(nc.sbuf_tensor("arena", [P, ARENA], F32))
        used = [0]

        def at(name, offset, shape, dtype):
            return nc.alloc_sbuf_tensor_at(name, shape, dtype, offset=base + offset)

        def take(name, shape, dtype):
            size = 4 * int(np.prod(shape[1:]))
            t = at(name, used[0], shape, dtype)
            places[name] = used[0]
            used[0] += (size + 31) // 32 * 32
            assert used[0] <= ARENA * 4, (name, used[0])
            return t

        places = {}
        H = take("residual", [P, DT, SEQ], F32)
        WTAIL = take("weight_tail", [P, RING, UNIT], F32R)
        WRAW = at("weight_raw", places["weight_tail"], [P, RING, UNIT], F32)
        WHEAD = take("weight_head", [P, RING, UNIT], F32R)
        U = take("norm_in", [P, DT, 2 * SEQ], F32R)
        Y = take("mixed", [P, 24, 2 * SEQ], F32R)
        TMP = take("half", [P, 4, SEQ], F32)
        YP = take("padded", [P, 4, SEQ + 4], F32)
        ACC = take("conv_acc", [P, 4, SEQ], F32)
        SG = take("gate", [P, 4, SEQ], F32)
        BC = take("bc", [P, 8, SEQ], F32)
        CA = take("ca", [P, 8, SEQ], F32)
        PAR = take("params", [P, PTILES * P], F32)
        IDENT = take("ident", [P, P], F32)
        ONES = take("ones", [P, P], F32)
        TRI = take("tri", [P, P], F32)
        UST = take("ust", [P, P], F32)
        MASK = at("causal", places["tri"], [P, 2 * P], F32)
        RSTD = take("rstd", [P, SEQ], F32)
        STAT = take("stat", [P, SEQ], F32)
        SQ = take("squares", [P, SEQ], F32)
        COS = take("cos", [P, SEQ], F32)
        SIN = take("sin", [P, SEQ], F32)
        CMPM = take("cmp_mask", [P, NT, NCMP], F32)
        CMP1 = take("cmp_keep", [P, NT, NCMP], F32)
        SMALL = take("small", [P, 672], F32)

        ZX = at("zx", places["mixed"], [P, 24, 2 * SEQ], F32)
        XST = at("x_stage", places["mixed"], [P, NT, D], F32)
        PST = at("param_stage", places["mixed"] + 16384, [P, PTILES, P], F32)
        CP = at("conf_pad", places["mixed"] + 16 * 2048, [P, 8, 2 * SEQ], F32)
        WS_RAW = at("ws_raw", places["bc"], [P, DT, NGATE], F32)
        WS_TAIL = at("ws_tail", places["bc"], [P, DT, NGATE], F32R)
        WS_HEAD = at("ws_head", places["bc"] + 4 * DT * NGATE, [P, DT, NGATE], F32R)
        XDT = at("x_dt", places["norm_in"], [P, NT, D], F32)
        LAT = at("la_tri", places["norm_in"] + 16384, [P, HPG * P], F32)
        DEC = at("decay", places["norm_in"] + 20480, [P, 2, HPG * P], F32)
        CE = at("c_exp", places["norm_in"] + 28672, [P, HPG * P], F32)
        VTOK = at("v_tok", places["norm_in"], [P, NT, 8, HD], F32)
        PROB = at("prob", places["norm_in"] + 8192, [P, 3, 528], F32)
        PT = at("prob_t", places["norm_in"] + 16384, [P, 2, 512], F32)
        PTC = at("prob_tc", places["norm_in"] + 20480, [P, 2, P], F32)
        W1 = at("w1", places["mixed"], [P, CB, HD], F32)
        BLK = at("blk", places["ca"], [P, CB, KVH * NCMP], F32)
        OST = at("out_stage", places["norm_in"], [P, NT, D], F32)
        YV = at("y_var", places["norm_in"], [P, GROUPS, SEQ], F32)
        YS = at("y_root", places["norm_in"] + 4096, [P, GROUPS, SEQ], F32)
        YT = at("y_newton", places["norm_in"] + 8192, [P, GROUPS, SEQ], F32)
        YN = at("y_normed", places["norm_in"] + 16384, [P, SSM_TILES, SEQ], F32)

        ROOT, NEWT = TMP[:, 0, :], TMP[:, 1, :]
        DTB, ALG = SMALL[:, 0:32], SMALL[:, 32:64]
        AN = SMALL[:, 64:96]
        DSK = SMALL[:, 96:112]
        DTV = SMALL[:, 112:176]
        LA = SMALL[:, 176:240]
        DTE = SMALL[:, 240:272]
        S1, S2, S3, S4 = (SMALL[:, 272 + 64 * i:336 + 64 * i] for i in range(4))
        RTOK = SMALL[:, 528:530]
        INV = SMALL[:, 640:641]
        BTOK = at("b_tok", places["conv_acc"], [P, GROUPS, STATE], F32)
        ST = at("state", places["conv_acc"] + 2048, [P, HPG * HP], F32)
        XD2 = at("x_dt_end", places["half"], [P, HPG * HP], F32)
        CBM = at("cb_masked", places["half"] + 2048, [P, P], F32)
        DALL = SMALL[:, 112:144]
        POSI = at("pos_i", places["small"] + 4 * 384, [P, SEQ], I32)
        GT = SMALL[:, 0:96]
        MX, SUMS, FAC = SMALL[:, 96:104], SMALL[:, 104:112], SMALL[:, 112:120]
        KCR = SMALL[:, 128:188]
        S1K, KSW, KC0 = SMALL[:, 192:252], SMALL[:, 256:316], SMALL[:, 320:380]
        W2 = SQ[:, :]
        VCT = SG[0:NCMP, 2:4, :].rearrange("p a b -> p (a b)")

        bank = [stack.enter_context(nc.psum_tensor(f"bank{i}", [P, 512], F32)) for i in range(8)]

        def sem(name):
            return stack.enter_context(nc.semaphore(name))

        x_landed, par_landed, misc_landed = sem("x_landed"), sem("par_landed"), sem("misc_landed")
        raw_landed = [sem(f"raw_landed{i}") for i in range(RING)]
        ws_landed, w1_landed, w2_landed = sem("ws_landed"), sem("w1_landed"), sem("w2_landed")
        stored = sem("stored")
        heads_ready = sem("heads_ready")
        tails_ready = sem("tails_ready")
        cols_done = sem("cols_done")
        half_copied = sem("half_copied")
        bank_read = sem("bank_read")
        scaled = sem("scaled")
        tap0 = sem("tap0")
        tap1, tap2, taps_done = sem("tap1"), sem("tap2"), sem("taps_done")
        silu_done, gated = sem("silu_done"), sem("gated")
        hid_head, hid_ready = sem("hid_head"), sem("hid_ready")
        half_added = sem("half_added")
        u_head, u_ready = sem("u_head"), sem("u_ready")
        sq_done, stat_added = sem("sq_done"), sem("stat_added")
        stat_summed, var_ready, root_ready = sem("stat_summed"), sem("var_ready"), sem("root_ready")
        rstd_ready = sem("rstd_ready")
        consts = sem("consts")
        turned, turned_read = sem("turned"), sem("turned_read")
        pturned, pturned_read = sem("pturned"), sem("pturned_read")
        dve_step, act_step, pool_step = sem("dve_step"), sem("act_step"), sem("pool_step")
        ws_head_ready, ws_ready, ws_done, rtok_turned = sem("ws_head"), sem("ws_ready"), sem("ws_done"), sem("rtok_turned")
        angles_ready, tables_ready = sem("angles_ready"), sem("tables_ready")
        x_ready = sem("x_ready")
        conf_in = sem("conf_in")
        conf_t0, conf_dve, conf_pool = sem("conf_t0"), sem("conf_dve"), sem("conf_pool")
        y_ready = sem("y_ready")
        ln_sum, ln_mean, ln_sub, ln_sq, ln_var, ln_silu, ln_norm = (sem(n) for n in (
            "ln_sum", "ln_mean", "ln_sub", "ln_sq", "ln_var", "ln_silu", "ln_norm"))
        xt_turned, xdt_ready, bt_turned, btok_ready = (sem(n) for n in ("xt_turned", "xdt_ready", "bt_turned", "btok_ready"))
        la_ready, dte_sum, dte_ready, xd2_ready, st_done, st_ready = (sem(n) for n in (
            "la_ready", "dte_sum", "dte_ready", "xd2_ready", "st_done", "st_ready"))
        lat_ready, d_done, e_done, cb_done, cbm_ready, dec_ready, ce_ready, m_ready, ssd_y, y_read = (
            sem(n) for n in ("lat_ready", "d_done", "e_done", "cb_done", "cbm_ready", "dec_ready",
                             "ce_ready", "m_ready", "ssd_y", "y_read"))
        yz_ready, ysq_ready, ynorm_sum, ynorm_var, ynorm_root, ynormed, y_head = (sem(n) for n in (
            "yz_ready", "ysq_ready", "ynorm_sum", "ynorm_var", "ynorm_root", "ynormed", "y_head"))
        glu_gate, conv_in, gates_in, rope_in, gates_ready = (sem(n) for n in (
            "glu_gate", "conv_in", "gates_in", "rope_in", "gates_ready"))
        dt_in, dt_exp, dtok_ready = sem("dt_in"), sem("dt_exp"), sem("dtok_ready")
        yc_ready, yc_head, o_head = sem("yc_ready"), sem("yc_head"), sem("o_head")
        swap_ready, kv_ready = sem("swap_ready"), sem("kv_ready")
        vt_turned, vt_ready = sem("vt_turned"), sem("vt_ready")
        blk_ready, h1_done, s1_ready, kc_done, kc_ready, vc_ready = (sem(n) for n in (
            "blk_ready", "h1_done", "s1_ready", "kc_done", "kc_ready", "vc_ready"))
        s_done, s_read, mx_ready, p_ready, pn_ready, pt_done, pt_read, o_done, o_read = (sem(n) for n in (
            "s_done", "s_read", "mx_ready", "p_ready", "pn_ready", "pt_done", "pt_read", "o_done", "o_read"))
        out_scaled, out_turned, out_read = sem("out_scaled"), sem("out_turned"), sem("out_read")
        store_ready = sem("store_ready")
        tap1_mlp, mask_ready = sem("tap1_mlp"), sem("mask_ready")

        def col(name, i=0):
            return PAR[:, PARAMS[name][0] + i:PARAMS[name][0] + i + 1]

        def dcol(name, i):
            return PAR[:, ds(i + PARAMS[name][0], 1)]

        block = stack.enter_context(nc.Block())

        @block.sync
        def _(sp):
            for t in range(NT):
                sp.dma_start(XST[:, t, :], x[0, t * P:(t + 1) * P, :]).then_inc(x_landed, 16)

            def load_group(weights, s4, units, kt, column):
                for u in range(units):
                    if not (isinstance(s4, int) and s4 == 0 and u < RING):
                        sp.wait_ge(cols_done, s4 * (4 * RING) + 4 * (u - RING + 1))
                    src = weights[u * kt * P:(u + 1) * kt * P, column].rearrange("(k p) n -> p k n", p=P)
                    dst = WRAW[:, u % RING, 0:kt * CW].rearrange("p (k n) -> p k n", k=kt)
                    sp.dma_start(dst, src).then_inc(raw_landed[u % RING], 16)

            def load_groups(weights, s, first, n, column):
                step, a = s.units // RING, s.unit // RING + first * (s.units // RING)
                if n > 2:
                    with sp.Fori(0, n) as i:
                        load_group(weights, i * step + a, s.units, s.kt, ds(i * CW + column, CW))
                else:
                    for i in range(n):
                        load_group(weights, i * step + a, s.units, s.kt, ds(i * CW + column, CW))

            def load_mlp(layer):
                up, down = ffn_w_up[layer], ffn_w_down[layer]
                for b, (h0, n) in enumerate(CHUNKS):
                    s = SPANS[f"up{layer}{b}"]
                    with sp.Fori(0, n // 4) as i:
                        for half in range(2):
                            load_group(up, i * 2 + s.unit // RING + half, 4, 4,
                                       ds(i * CW + h0 * P + half * FF, CW))
                    load_groups(down[h0 * P:(h0 + n) * P, :], SPANS[f"down{layer}{b}"], 0, 4, 0)

            s = SPANS["in0"]
            w = ab_w_in[0]
            load_group(w, 0, 4, 4, ds(GLUC, CW))
            sp.dma_start(WS_RAW[:, :, 0:HEADS], w[:, DTC:DTC + HEADS].rearrange("(k p) n -> p k n", p=P))\
              .then_inc(ws_landed, 16)
            load_groups(w, s, 1, 3, GLUC + CW)
            load_groups(w, s, 4, 2, XBCC + D)
            load_groups(w, s, 6, 4, XBCC)
            load_groups(w, s, 10, 4, ZC)
            load_groups(ab_w_out[0], SPANS["out0"], 0, 4, 0)
            load_mlp(0)
            s = SPANS["in1"]
            w = cd_w_in[0]
            sp.dma_start(WS_RAW[:, :, :], w[:, GATEC:GATEC + NGATE].rearrange("(k p) n -> p k n", p=P))\
              .then_inc(ws_landed, 16)
            load_groups(w, s, 0, 2, KVC)
            sp.dma_start(W1[:, :, :], nsa_cmp_w1[0, 0].rearrange("(l d) o -> d l o", d=HD)).then_inc(w1_landed, 16)
            load_groups(w, s, 2, 4, KVC + 2 * CW)
            load_groups(w, s, 6, 4, QC)
            load_groups(w, s, 10, 4, SC)
            load_groups(w, s, 14, 2, 0)
            load_groups(cd_w_out[0], SPANS["out1"], 0, 4, 0)
            load_mlp(1)
            for t in range(NT):
                sp.wait_ge(store_ready, 2 * (t + 1))
                sp.wait_ge(out_read, 2 * (t + 1))
                sp.dma_start(out[0, t * P:(t + 1) * P, :], OST[:, t, :]).then_inc(stored, 16)
            sp.wait_ge(stored, 16 * NT)

        @block.gpsimd
        def _(pool):
            steps = [0]

            def link(ins):
                steps[0] += 1
                ins.then_inc(pool_step, 1)
                pool.wait_ge(pool_step, steps[0])

            link(pool.memset(IDENT[:, :], 0.0))
            pool.affine_select(out=IDENT[:, :], in_=IDENT[:, :], compare_op=ALU.not_equal, fill=1.0, base=0,
                               pattern=[[-1, P]], channel_multiplier=1).then_inc(consts, 1)
            pool.memset(ONES[:, :], 1.0).then_inc(consts, 1)
            pool.memset(YP[:, :, :], 0.0).then_inc(consts, 1)
            pool.memset(CP[:, :, 0:CONF_TAPS - 1], 0.0).then_inc(consts, 1)
            pool.wait_ge(consts, 4)
            pool.affine_select(out=TRI[:, :], in_=ONES[:, :], compare_op=ALU.is_ge, fill=0.0, base=0,
                               pattern=[[1, P]], channel_multiplier=-1).then_inc(consts, 1)
            pool.affine_select(out=UST[:, :], in_=ONES[:, :], compare_op=ALU.is_gt, fill=0.0, base=0,
                               pattern=[[-1, P]], channel_multiplier=1).then_inc(consts, 1)
            link(pool.memset(CMPM[:, :, :], 0.0))
            link(pool.memset(CMP1[:, :, :], 1.0))
            for m, fill in ((CMPM, NEG), (CMP1, 0.0)):
                pool.affine_select(out=m[:, :, :], in_=m[:, :, :], compare_op=ALU.is_ge, fill=fill,
                                   base=1 - CB, pattern=[[P, NT], [-CSTRIDE, NCMP]],
                                   channel_multiplier=1).then_inc(consts, 1)
            counts = {"sq": 0, "stat": 0}

            def statistics(tile):
                pool.tensor_tensor(SQ[:, :], H[:, tile, :], H[:, tile, :], ALU.mult).then_inc(sq_done, 1)
                counts["sq"] += 1
                pool.wait_ge(sq_done, counts["sq"])
                if tile == 0:
                    pool.tensor_copy(STAT[:, :], SQ[:, :]).then_inc(stat_added, 1)
                else:
                    pool.tensor_tensor(STAT[:, :], STAT[:, :], SQ[:, :], ALU.add).then_inc(stat_added, 1)
                counts["stat"] += 1
                pool.wait_ge(stat_added, counts["stat"])

            def norm_statistics(n, s):
                if n:
                    pool.wait_ge(stat_summed, n)
                for tile in range(DT):
                    if s is None:
                        pool.wait_ge(turned_read, tile // 2 + 1)
                    else:
                        pool.wait_ge(bank_read, s.tile + tile + 1)
                    statistics(tile)

            norm_statistics(0, None)
            for m in range(POOL_CONF):
                j = CONF_TILES - POOL_CONF + m
                pool.wait_ge(conf_t0, j + 1)
                for k in range(CONF_TAPS - 1):
                    link(pool.tensor_scalar(SQ[:, :], CP[:, j, k:k + SEQ], col("dw_w", k * CONF_TILES + j), 0.0,
                                            ALU.mult, ALU.add))
                    link(pool.tensor_tensor(CA[:, j, :], CA[:, j, :], SQ[:, :], ALU.add))
                pool.tensor_copy(CA[:, j, :], CA[:, j, :]).then_inc(conf_pool, 1)
            for g in range(GROUPS):
                pool.wait_ge(yz_ready, g + 1)
                z, y = ZX[:, 4 * g:4 * g + 4, 0:SEQ], ZX[:, 4 * g:4 * g + 4, SEQ:2 * SEQ]
                link(pool.tensor_tensor(z, y, y, ALU.mult))
                link(pool.tensor_tensor(ZX[:, 4 * g:4 * g + 2, 0:SEQ], ZX[:, 4 * g:4 * g + 2, 0:SEQ],
                                        ZX[:, 4 * g + 2:4 * g + 4, 0:SEQ], ALU.add))
                pool.tensor_tensor(ZX[:, 4 * g, 0:SEQ], ZX[:, 4 * g, 0:SEQ], ZX[:, 4 * g + 1, 0:SEQ],
                                   ALU.add).then_inc(ysq_ready, 1)
            norm_statistics(1, SPANS["out0"])
            link(pool.memset(MASK[:, :], 0.0))
            pool.affine_select(out=MASK[:, P:2 * P], in_=MASK[:, P:2 * P], compare_op=ALU.is_ge, fill=NEG,
                               base=0, pattern=[[-1, P]], channel_multiplier=1).then_inc(mask_ready, 1)
            norm_statistics(2, SPANS["down02"])
            norm_statistics(3, SPANS["out1"])
            norm_statistics(4, SPANS["down12"])

        @block.scalar
        def _(act):
            rows = (("mix", mix_norm.rearrange("a (t p) -> (a t) p", p=P)),
                    ("ffn", ffn_norm.rearrange("a (t p) -> (a t) p", p=P)),
                    ("final", final_norm.rearrange("(t p) -> t p", p=P)),
                    ("sconv_w", ssm_conv_w[0].rearrange("a (t p) -> (a t) p", p=P)),
                    ("sconv_b", ssm_conv_b[0].rearrange("(t p) -> t p", p=P)),
                    ("snorm", ssm_norm[0].rearrange("(t p) -> t p", p=P)),
                    ("dw_w", conf_dw_w[0].rearrange("a (t p) -> (a t) p", p=P)),
                    ("dw_b", conf_dw_b[0].rearrange("(t p) -> t p", p=P)),
                    ("ln_g", conf_ln_g[0].rearrange("(t p) -> t p", p=P)),
                    ("ln_b", conf_ln_b[0].rearrange("(t p) -> t p", p=P)),
                    ("sc_w", sc_conv_w[0].rearrange("a (t p) -> (a t) p", p=P)),
                    ("pe", nsa_cmp_pe[0].rearrange("a l p -> (a l) p")),
                    ("fconv_w", ffn_conv_w.rearrange("l a (t p) -> (l a t) p", p=P)),
                    ("fconv_b", ffn_conv_b.rearrange("l (t p) -> (l t) p", p=P)))
            loads = 0
            for name, src in rows:
                c0, n = PARAMS[name]
                r = 0
                while r < n:
                    tile, row = divmod(c0 + r, P)
                    k = min(n - r, P - row)
                    act.dma_start(PST[row:row + k, tile, :], src[r:r + k, :]).then_inc(par_landed, 16)
                    r, loads = r + k, loads + 1
            act.dma_start(DTB, ssm_dt_bias[0:1, :].to_broadcast([P, HEADS])).then_inc(misc_landed, 16)
            act.dma_start(ALG, ssm_a_log[0:1, :].to_broadcast([P, HEADS])).then_inc(misc_landed, 16)
            act.dma_start(DALL, ssm_d[0:1, :].to_broadcast([P, HEADS])).then_inc(misc_landed, 16)
            act.dma_start(POSI[:, :], positions[0:1, :].to_broadcast([P, SEQ])).then_inc(misc_landed, 16)
            act.dma_start(INV, inv_freq).then_inc(misc_landed, 16)
            assert loads == PAR_LOADS

            steps = [0]

            def link(ins):
                steps[0] += 1
                ins.then_inc(act_step, 1)
                act.wait_ge(act_step, steps[0])

            def heads(s4, off, kt=4):
                act.wait_ge(raw_landed[off % RING], s4 * 16 + 16 * (off // RING + 1))
                act.activation(WHEAD[:, off % RING, 0:kt * CW], WRAW[:, off % RING, 0:kt * CW], ACT.Copy)\
                   .then_inc(heads_ready, 1)

            def copy_halves(e):
                for c in range(4):
                    act.wait_ge(cols_done, e * 4 + c - 3)
                    act.activation(TMP[:, c, :], bank[c][:, SEQ:2 * SEQ], ACT.Copy).then_inc(half_copied, 1)

            def u_heads(gain, tile):
                act.activation(U[:, tile, 0:SEQ], H[:, tile, :], ACT.Copy, scale=gain).then_inc(u_head, 1)

            def root(n):
                act.wait_ge(var_ready, n)
                act.activation(ROOT, RSTD[:, :], ACT.Sqrt).then_inc(root_ready, 1)
                act.wait_ge(rstd_ready, n)

            for b in range(-(-PTILES // 4)):
                act.wait_ge(pturned, b + 1)
                n = min(4, PTILES - 4 * b)
                w = min(n * P, NPARAM - 4 * b * P)
                act.activation(PAR[:, 4 * b * P:4 * b * P + w], bank[b][:, 0:w], ACT.Copy)\
                   .then_inc(pturned_read, 1)
            for off in range(2):
                heads(0, off)
            for tile in range(DT):
                if tile == 0:
                    act.wait_ge(pturned_read, -(-PTILES // 4))
                act.wait_ge(turned_read, tile // 2 + 1)
                u_heads(col("mix", tile), tile)
            heads(0, 2)
            heads(0, 3)
            root(1)
            act.wait_ge(angles_ready, 1)
            act.activation(SIN[:, :], SIN[:, :], ACT.Sin).then_inc(tables_ready, 1)
            act.activation(COS[:, :], COS[:, :], ACT.Sin).then_inc(tables_ready, 1)
            heads(0, 4)
            heads(0, 5)

            def mlp(layer):
                for b, (h0, n) in enumerate(CHUNKS):
                    s, gate0 = SPANS[f"up{layer}{b}"], layer * FT + h0
                    plain, conv = PLAIN[f"up{layer}{b}"], CONV[f"up{layer}{b}"]

                    def turn(i, turns):
                        for half in range(2):
                            first = s.unit + 4 * half + 4
                            kts = ahead(first + (8 * i if turns == 1 else 0), 8, turns)
                            e = i * 8 + first
                            e4 = i * 2 + (s.unit // RING + half + 1)
                            copy_halves(e)
                            heads(e4, 2, kts[0])
                            for c in range(4):
                                k = i * 8 + (4 * half + c + 1)
                                t = i * 4 + (h0 + c + half * FT)
                                act.wait_ge(scaled, k + plain)
                                act.activation(ACC[:, c, :], YP[:, c, 3:3 + SEQ], ACT.Identity,
                                               bias=dcol("fconv_b", t + layer * 2 * FT),
                                               scale=dcol("fconv_w", t + (layer * 3 + 2) * 2 * FT))\
                                   .then_inc(tap0, 1)
                            heads(e4, 3, kts[1])
                            for c in range(4):
                                if half == 0:
                                    act.wait_ge(taps_done, i * 8 + (conv + c + 1))
                                    act.activation(SG[:, c, :], ACC[:, c, :], ACT.Silu).then_inc(silu_done, 1)
                                else:
                                    act.wait_ge(gated, i * 4 + (gate0 + c + 1))
                                    act.activation(Y[:, ds(i * 4 + c, 1), 0:SEQ], ACC[:, c:c + 1, :], ACT.Copy)\
                                       .then_inc(hid_head, 1)
                            heads(e4, 4, kts[2])
                            heads(e4, 5, kts[3])

                    turns = n // 4 - (b == len(CHUNKS) - 1)
                    with act.Fori(0, turns) as i:
                        turn(i, turns)
                    if turns < n // 4:
                        turn(turns, 1)
                    s = SPANS[f"down{layer}{b}"]
                    last = b == len(CHUNKS) - 1
                    norm = 2 * layer + 2
                    if last:
                        gain = ("mix", DT) if layer == 0 else None
                        residual_groups(s, 2, gain)
                        for i in (2, 3):
                            e = s.unit + 4 * (i + 1)
                            residual_group(s.tile + 4 * i, e, e // RING, i, gain, rest(e))
                    else:
                        residual_groups(s, 4, None)
                    if last:
                        root(norm + 1)

            def residual_group(t, e, e4, i, gain, kts):
                for k, kt in enumerate(kts):
                    heads(e4, k + 2, kt)
                    if k == 0 and gain is not None:
                        for c in range(4):
                            act.wait_ge(bank_read, t + c + 1)
                            tile = i * 4 + c
                            act.activation(U[:, ds(tile, 1), 0:SEQ], H[:, ds(tile, 1), :], ACT.Copy,
                                           scale=dcol(gain[0], i * 4 + (c + gain[1]))).then_inc(u_head, 1)

            def residual_groups(s, n, gain):
                kts = ahead(s.unit + s.units, s.units, n)
                with act.Fori(0, n) as i:
                    residual_group(i * 4 + s.tile, i * s.units + (s.unit + s.units),
                                   i * (s.units // RING) + (s.unit + s.units) // RING, i, gain, kts)

            def out_projection(layer):
                s = SPANS[f"out{layer}"]
                for i in range(s.groups):
                    e = s.unit + (i + 1) * s.units
                    kts = ahead(e, 0, 1, range(2, 10 if i < 3 else 6))
                    residual_group(s.tile + 4 * i, e, e // RING, i, ("ffn", layer * DT), kts)
                root(2 * layer + 2)

            def small_heads(n):
                act.wait_ge(ws_landed, 16 * (1 if n == HEADS else 2))
                act.activation(WS_HEAD[:, :, 0:n], WS_RAW[:, :, 0:n], ACT.Copy).then_inc(ws_head_ready, 1)

            s, conv, ready = SPANS["in0"], 0, 0
            small_heads(HEADS)
            for q in range(s.groups):
                e = s.unit + 4 * (q + 1)
                last = q == s.groups - 1
                copy_halves(e)
                kts = ahead(e, 0, 1)
                heads(e // RING, 2, kts[0])
                for c in range(4):
                    done = PLAIN["in0"] + 4 * q + c + 1
                    if 4 <= q < 10:
                        j = (16 + 4 * (q - 4) if q < 6 else 4 * (q - 6)) + c
                        act.wait_ge(scaled, done)
                        act.activation(ACC[:, c, :], YP[:, c, 3:3 + SEQ], ACT.Identity,
                                       bias=col("sconv_b", j), scale=col("sconv_w", 3 * 24 + j)).then_inc(tap0, 1)
                heads(e // RING, 3, kts[1])
                for c in range(4):
                    done = PLAIN["in0"] + 4 * q + c + 1
                    if 2 <= q < 4:
                        act.wait_ge(scaled, done)
                        act.activation(SG[:, c, :], YP[:, c, 3:3 + SEQ], ACT.Sigmoid).then_inc(glu_gate, 1)
                    elif 4 <= q < 10:
                        conv += 1
                        act.wait_ge(taps_done, conv)
                        dst = BC[:, 4 * (q - 4) + c, :] if q < 6 else ZX[:, 4 * (q - 6) + c, SEQ:2 * SEQ]
                        act.activation(dst, ACC[:, c, :], ACT.Silu).then_inc(x_ready, 1)
                    elif q >= 10:
                        act.wait_ge(scaled, done)
                        act.activation(ZX[:, 4 * (q - 10) + c, 0:SEQ], YP[:, c, 3:3 + SEQ], ACT.Silu)\
                           .then_inc(x_ready, 1)
                if q in (2, 3):
                    for c in range(4):
                        j = 4 * (q - 2) + c
                        act.wait_ge(conf_in, j + 1)
                        act.activation(CA[:, j, :], CP[:, j, CONF_TAPS - 1:CONF_TAPS - 1 + SEQ], ACT.Identity,
                                       bias=col("dw_b", j), scale=col("dw_w", (CONF_TAPS - 1) * CONF_TILES + j))\
                           .then_inc(conf_t0, 1)
                if not last:
                    heads(e // RING, 4, kts[2])
                    heads(e // RING, 5, kts[3])
                if q == 1:
                    act.wait_ge(dt_in, 1)
                    act.activation(S2, S2, ACT.Exp).then_inc(dt_exp, 1)
                    act.wait_ge(misc_landed, 16 * 5)
                    act.activation(AN, ALG, ACT.Exp).then_inc(dt_exp, 1)

            act.wait_ge(ln_sum, 1)
            act.activation(TMP[:, 3, :], bank[0][:, 0:SEQ], ACT.Copy, scale=1.0 / (CONF_TILES * P)).then_inc(ln_mean, 1)
            act.wait_ge(ln_sub, 1)
            act.activation(CP[:, :, 0:SEQ], CA[:, :, :], ACT.Square).then_inc(ln_sq, 1)
            act.wait_ge(ln_var, 1)
            act.activation(ROOT, TMP[:, 3, :], ACT.Sqrt).then_inc(ln_var, 1)
            for j in range(CONF_TILES):
                act.wait_ge(ln_norm, j + 1)
                act.activation(CA[:, j, :], CA[:, j, :], ACT.Silu, bias=col("ln_b", j)).then_inc(ln_silu, 1)
            act.wait_ge(ln_silu, CONF_TILES)
            act.activation(Y[:, SSM_TILES:SSM_TILES + CONF_TILES, 0:SEQ], CA[:, :, :], ACT.Copy).then_inc(ln_mean, 1)

            act.wait_ge(bt_turned, 1)
            act.activation(BTOK[:, :, :], bank[2][:, :].rearrange("p (g n) -> p g n", g=GROUPS), ACT.Copy)\
               .then_inc(btok_ready, 1)
            act.wait_ge(dte_sum, 1)
            act.activation(DTE, bank[3][:, 0:HEADS], ACT.Exp).then_inc(dte_ready, 1)
            for m in range(2 * GROUPS):
                g, chunk = divmod(m, 2)
                act.wait_ge(d_done, m + 1)
                if m >= 2:
                    act.wait_ge(ssd_y, m - 1)
                for h in range(2):
                    act.activation(DEC[:, m % 2, h * 512:(h + 1) * 512], bank[4 + h][:, :], ACT.Exp).then_inc(dec_ready, 1)
                if chunk == 0:
                    act.wait_ge(st_done, g + 1)
                    if g:
                        act.wait_ge(ssd_y, 2 * g)
                    act.activation(ST[:, :], bank[3][:, :], ACT.Copy).then_inc(st_ready, 1)
                else:
                    act.wait_ge(e_done, g + 1)
                    if g:
                        act.wait_ge(ssd_y, 2 * g)
                    for h in range(2):
                        act.activation(CE[:, h * 512:(h + 1) * 512], bank[h][:, :], ACT.Exp).then_inc(dec_ready, 1)
            act.wait_ge(ynorm_var, 1)
            act.activation(YS[:, :, :], YV[:, :, :], ACT.Sqrt).then_inc(ynorm_root, 1)
            for g in range(GROUPS):
                act.wait_ge(ynormed, 4 * g + 4)
                act.activation(Y[:, 4 * g:4 * g + 4, 0:SEQ], YN[:, 4 * g:4 * g + 4, :], ACT.Copy).then_inc(y_head, 1)
            e = SPANS["out0"].unit
            for k in range(4, 10):
                heads(e // RING, k, kt_at(e + k))
            out_projection(0)
            mlp(0)

            s = SPANS["in1"]
            small_heads(NGATE)
            swaps = 0

            def compress_silu(i):
                act.wait_ge(h1_done, i + 1)
                if i == 0:
                    act.dma_start(W1[:, :, :], nsa_cmp_w1[0, 1].rearrange("(l d) o -> d l o", d=HD))\
                       .then_inc(w1_landed, 16)
                act.activation(S1K, bank[4][:, 0:KVH * NCMP], ACT.Silu).then_inc(s1_ready, 1)

            def compressed_k():
                act.wait_ge(kc_done, 1)
                act.activation(KC0, bank[5][:, 0:KVH * NCMP], ACT.Copy).then_inc(kc_ready, 1)
                act.activation(KSW[0:64, :], bank[5][64:128, 0:KVH * NCMP], ACT.Copy).then_inc(kc_ready, 1)
                act.activation(KSW[64:128, :], bank[5][0:64, 0:KVH * NCMP], ACT.Copy).then_inc(kc_ready, 1)

            def compressed_v():
                act.wait_ge(kc_done, 2)
                act.wait_ge(kv_ready, 4 * 6 + 1)
                act.activation(VCT, bank[5][0:NCMP, 0:KVH * HD], ACT.Copy).then_inc(vc_ready, 1)

            for q in range(s.groups):
                e = s.unit + 4 * (q + 1)
                copy_halves(e)
                kts = ahead(e, 0, 1)
                heads(e // RING, 2, kts[0])
                if q in (2, 4, 6, 7, 8, 9):
                    for c in range(4):
                        act.wait_ge(scaled, PLAIN["in1"] + 4 * q + c + 1)
                        act.activation(SG[0:64, c, :], YP[64:128, c, 3:3 + SEQ], ACT.Copy).then_inc(swap_ready, 1)
                        act.activation(SG[64:128, c, :], YP[0:64, c, 3:3 + SEQ], ACT.Copy).then_inc(swap_ready, 1)
                if q in (12, 13):
                    for c in range(4):
                        j = 4 * (q - 12) + c
                        act.wait_ge(conv_in, j + 1)
                        act.activation(ACC[:, c, :], YP[:, c, 3:3 + SEQ], ACT.Copy,
                                       scale=col("sc_w", 2 * 8 + j)).then_inc(tap0, 1)
                heads(e // RING, 3, kts[1])
                if q in (14, 15):
                    act.wait_ge(yc_ready, 4 * (q - 13))
                    act.activation(Y[:, 4 * (q - 14):4 * (q - 14) + 4, 0:SEQ], ACC[:, :, :], ACT.Copy)\
                       .then_inc(yc_head, 1)
                if q == 1:
                    act.wait_ge(gates_in, 1)
                    act.activation(GT, GT, ACT.Sigmoid).then_inc(gates_ready, 1)
                    act.dma_start(W2.rearrange("p (i n) -> p i n", i=2), nsa_cmp_w2[0].rearrange("i p n -> p i n"))\
                       .then_inc(w2_landed, 16)
                if q == COMPRESS[0] + 1:
                    compress_silu(0)
                if q == COMPRESS[1] + 1:
                    compressed_k()
                    compress_silu(1)
                if q == 10:
                    compressed_v()
                if q < s.groups - 1:
                    heads(e // RING, 4, kts[2])
                    heads(e // RING, 5, kts[3])

            for k in range(4):
                act.wait_ge(vt_turned, k + 1)
                act.activation(VTOK[:, k % 2, 4 * (k // 2):4 * (k // 2) + 4, :],
                               bank[4 + k][:, :].rearrange("p (g d) -> p g d", g=KVH), ACT.Copy).then_inc(vt_ready, 1)
            last = NSA_HEADS * NT
            for n in range(last + 4):
                if 2 <= n < last + 2:
                    m = n - 2
                    blocks = 2 * (m % NT + 1)
                    act.wait_ge(pt_done, m + 1)
                    if m >= 2:
                        act.wait_ge(o_done, m - 1)
                    act.activation(PT[:, m % 2, 0:blocks * P], bank[4 + m % 2][:, 0:blocks * P], ACT.Copy).then_inc(pt_read, 1)
                    act.activation(PTC[0:NCMP, m % 2, :], bank[3 - m % 2][0:NCMP, P:2 * P], ACT.Copy).then_inc(pt_read, 1)
                if n < last:
                    b, p3, nk = n % 2, n % 3, P * (n % NT + 1)
                    act.wait_ge(mx_ready, n + 1)
                    for r, probs in enumerate((PROB[:, p3, 512:512 + NCMP], PROB[:, p3, 0:nk], PROB[:, p3, SEQ:SEQ + nk])):
                        act.activation(probs, probs, ACT.Exp, bias=MX[:, 4 * b + r:4 * b + r + 1], scale=SCALE,
                                       accum_out=SUMS[:, 4 * b + r:4 * b + r + 1]).then_inc(p_ready, 1)
                if n >= 4:
                    m = n - 4
                    h, t = divmod(m, NT)
                    act.wait_ge(o_done, m + 1)
                    act.activation(Y[:, 8 + h, t * P:(t + 1) * P], bank[6 + m % 2][:, 0:P], ACT.Copy).then_inc(o_head, 1)
            e = SPANS["out1"].unit
            for k in range(4, 10):
                heads(e // RING, k, kt_at(e + k))
            out_projection(1)
            mlp(1)

            for k in range(4 * NT):
                if k % 2:
                    act.wait_ge(out_turned, k + 1)
                    act.activation(OST[:, k // 4, (k % 4) * 512:(k % 4 + 1) * 512], bank[4 + k % 4][:, :], ACT.Copy)\
                       .then_inc(store_ready, 1)

        @block.vector
        def _(dve):
            steps = [0]

            def link(ins):
                steps[0] += 1
                ins.then_inc(dve_step, 1)
                dve.wait_ge(dve_step, steps[0])

            def tails(n, off, kt=4):
                dve.wait_ge(heads_ready, n + off + 1)
                dve.tensor_tensor(WTAIL[:, off % RING, 0:kt * CW], WRAW[:, off % RING, 0:kt * CW],
                                  WHEAD[:, off % RING, 0:kt * CW].bitcast(F32), ALU.subtract).then_inc(tails_ready, 1)

            def read_banks(plain, tile, dst):
                for c in range(4):
                    dve.wait_ge(half_copied, plain + c + 1)
                    dve.tensor_tensor(TMP[:, c, :], bank[c][:, 0:SEQ], TMP[:, c, :], ALU.add).then_inc(bank_read, 1)
                    dve.wait_ge(bank_read, tile + c + 1)
                    dve.tensor_tensor(dst(c), TMP[:, c, :], RSTD[:, :], ALU.mult).then_inc(scaled, 1)

            def data(c):
                return YP[:, c, 3:3 + SEQ]

            def back(c, k):
                return YP[:, c, 3 - k:3 - k + SEQ]

            def newton(v, y, t, result):
                link(dve.reciprocal(y, y))
                link(dve.tensor_tensor(t, y, y, ALU.mult))
                link(dve.tensor_tensor(t, t, v, ALU.mult))
                link(dve.tensor_scalar(t, t, -0.5, 1.5, ALU.mult, ALU.add))
                return dve.tensor_tensor(result, y, t, ALU.mult)

            def variance(n):
                dve.wait_ge(stat_summed, n)
                dve.tensor_scalar(RSTD[:, :], bank[4][:, 0:SEQ], 1.0 / D, EPS, ALU.mult, ALU.add).then_inc(var_ready, 1)

            def norm_factor(n):
                dve.wait_ge(root_ready, n)
                newton(RSTD[:, :], ROOT, NEWT, RSTD[:, :]).then_inc(rstd_ready, 1)
                dve.wait_ge(rstd_ready, n)

            for k in range(8):
                dve.wait_ge(turned, k + 1)
                dve.tensor_copy(H[:, 2 * k:2 * k + 2, :], bank[4 + k % 4][:, :].rearrange("p (j s) -> p j s", j=2))\
                   .then_inc(turned_read, 1)
            tails(0, 0)
            tails(0, 1)
            for tile in range(DT):
                dve.wait_ge(u_head, tile + 1)
                dve.scalar_tensor_tensor(out=U[:, tile, SEQ:2 * SEQ], in0=H[:, tile, :], scalar=col("mix", tile),
                                         in1=U[:, tile, 0:SEQ].bitcast(F32), op0=ALU.mult, op1=ALU.subtract)\
                   .then_inc(u_ready, 1)
            tails(0, 2)
            tails(0, 3)
            dve.wait_ge(misc_landed, 16 * 5)
            for r in range(2):
                half = slice(HP * r, HP * (r + 1))
                link(dve.tensor_copy(DSK[half, :], DALL[half, r:HEADS:2]))
            variance(1)

            dve.wait_ge(misc_landed, 16 * 5)
            a, k = ACC[:, 1, :], ACC[:, 2, :]
            link(dve.tensor_copy(ACC[:, 0, :], POSI[:, :]))
            link(dve.tensor_scalar(a, ACC[:, 0, :], INV, None, ALU.mult))
            link(dve.tensor_scalar(k, a, float(0.5 / np.pi), ROUNDER, ALU.mult, ALU.add))
            link(dve.tensor_scalar(k, k, ROUNDER, None, ALU.subtract))
            for part in TURN:
                link(dve.scalar_tensor_tensor(out=a, in0=k, scalar=-part, in1=a, op0=ALU.mult, op1=ALU.add))
            link(dve.tensor_scalar(a, a, PI, -PI, ALU.min, ALU.max))
            link(dve.scalar_tensor_tensor(out=k, in0=a, scalar=-1.0, in1=a, op0=ALU.mult, op1=ALU.max))
            link(dve.tensor_scalar(SIN[0:64, :], a[0:64, :], -1.0, None, ALU.mult))
            link(dve.tensor_copy(SIN[64:128, :], a[64:128, :]))
            dve.tensor_scalar(COS[:, :], k, -1.0, float(np.float32(np.pi / 2)), ALU.mult, ALU.add).then_inc(angles_ready, 1)
            norm_factor(1)
            tails(0, 4)
            tails(0, 5)

            def small_tails(count, n):
                dve.wait_ge(ws_head_ready, count)
                dve.tensor_tensor(WS_TAIL[:, :, 0:n], WS_RAW[:, :, 0:n], WS_HEAD[:, :, 0:n].bitcast(F32),
                                  ALU.subtract).then_inc(ws_ready, 1)

            def small_scaled(count, n, dst):
                dve.wait_ge(rtok_turned, count)
                link(dve.tensor_copy(RTOK, bank[5][:, 0:2 * P:P]))
                for t in range(NT):
                    link(dve.tensor_scalar(dst[:, t * n:(t + 1) * n], bank[4][:, 64 * t:64 * t + n],
                                           RTOK[:, t:t + 1], None, ALU.mult))

            def step_sizes():
                small_scaled(1, HEADS, S1)
                for t in range(NT):
                    link(dve.tensor_tensor(S1[:, 32 * t:32 * t + 32], S1[:, 32 * t:32 * t + 32], DTB, ALU.add))
                dve.scalar_tensor_tensor(out=S2, in0=S1, scalar=-1.0, in1=S1, op0=ALU.mult, op1=ALU.min)\
                   .then_inc(dt_in, 1)
                dve.wait_ge(dt_exp, 2)
                link(dve.tensor_scalar(S3, S2, 2.0, None, ALU.add))
                link(dve.reciprocal(S3, S3))
                link(dve.tensor_tensor(S3, S2, S3, ALU.mult))
                link(dve.tensor_tensor(S4, S3, S3, ALU.mult))
                link(dve.tensor_scalar(S2, S4, 1.0 / 17, None, ALU.mult))
                for odd in (15, 13, 11, 9, 7, 5, 3):
                    link(dve.scalar_tensor_tensor(out=S2, in0=S2, scalar=1.0 / odd, in1=S4, op0=ALU.add, op1=ALU.mult))
                link(dve.tensor_scalar(S2, S2, 1.0, 2.0, ALU.add, ALU.mult))
                link(dve.tensor_tensor(S2, S2, S3, ALU.mult))
                link(dve.scalar_tensor_tensor(out=DTV, in0=S1, scalar=0.0, in1=S2, op0=ALU.max, op1=ALU.add))
                for t in range(NT):
                    r = slice(32 * t, 32 * t + 32)
                    dve.scalar_tensor_tensor(out=LA[:, r], in0=DTV[:, r], scalar=-1.0, in1=AN, op0=ALU.mult,
                                             op1=ALU.mult).then_inc(la_ready, 1)
                dve.wait_ge(la_ready, NT)

            small_tails(1, HEADS)
            s, conv, conf, n_conf = SPANS["in0"], 0, 0, CONF_TILES - POOL_CONF
            conf_ops = [(k, j) for k in range(CONF_TAPS - 1) for j in range(n_conf)]
            dve.wait_ge(consts, CONSTS)
            for q in range(s.groups):
                e, last = s.unit + 4 * (q + 1), q == s.groups - 1
                dst = data if q > 1 else lambda c: CA[:, 4 * q + c, :]
                read_banks(PLAIN["in0"] + 4 * q, s.tile + 4 * q, dst)
                kts = ahead(e, 0, 1)
                tails(e, 2, kts[0])
                if q in (2, 3):
                    for c in range(4):
                        j = 4 * (q - 2) + c
                        dve.wait_ge(glu_gate, j + 1)
                        dve.tensor_tensor(CP[:, j, CONF_TAPS - 1:CONF_TAPS - 1 + SEQ], CA[:, j, :], SG[:, c, :],
                                          ALU.mult).then_inc(conf_in, 1)
                if 4 <= q < 10:
                    j0 = 16 + 4 * (q - 4) if q < 6 else 4 * (q - 6)
                    for k, done in ((1, tap1), (2, tap2), (3, taps_done)):
                        before = (tap0, tap1, tap2)[k - 1]
                        for c in range(4):
                            dve.wait_ge(before, conv + c + 1)
                            dve.scalar_tensor_tensor(out=ACC[:, c, :], in0=back(c, k),
                                                     scalar=col("sconv_w", (3 - k) * 24 + j0 + c), in1=ACC[:, c, :],
                                                     op0=ALU.mult, op1=ALU.add).then_inc(done, 1)
                    conv += 4
                tails(e, 3, kts[1])
                if q == 1:
                    step_sizes()
                if q >= 4:
                    share = -(-len(conf_ops) // (s.groups - 4))
                    for k, j in conf_ops[conf:conf + share]:
                        if k == 0:
                            dve.wait_ge(conf_t0, j + 1)
                        else:
                            dve.wait_ge(conf_dve, conf + 1 - n_conf)
                        dve.scalar_tensor_tensor(out=CA[:, j, :], in0=CP[:, j, k:k + SEQ],
                                                 scalar=col("dw_w", k * CONF_TILES + j), in1=CA[:, j, :],
                                                 op0=ALU.mult, op1=ALU.add).then_inc(conf_dve, 1)
                        conf += 1
                if not last:
                    tails(e, 4, kts[2])
                    tails(e, 5, kts[3])

            dve.wait_ge(ln_mean, 1)
            dve.tensor_tensor(CA[:, :, :], CA[:, :, :], TMP[:, 3:4, :].to_broadcast([P, CONF_TILES, SEQ]),
                              ALU.subtract).then_inc(ln_sub, 1)

            def x_dt(k):
                g, t = divmod(k, 2)
                dve.wait_ge(xt_turned, k + 1)
                dve.tensor_tensor(XDT[:, t, g * 512:(g + 1) * 512].rearrange("p (h c) -> p h c", h=HPG),
                                  bank[4 + k % 4][:, :].rearrange("p (h c) -> p h c", h=HPG),
                                  DTV[:, 32 * t + HPG * g:32 * t + HPG * (g + 1)].unsqueeze(2).to_broadcast([P, HPG, HP]),
                                  ALU.mult).then_inc(xdt_ready, 1)

            for k in range(2 * GROUPS):
                x_dt(k)
            dve.wait_ge(ln_sum, 2)
            dve.tensor_scalar(TMP[:, 3, :], bank[1][:, 0:SEQ], 1.0 / (CONF_TILES * P), EPS, ALU.mult, ALU.add)\
               .then_inc(ln_var, 1)
            dve.wait_ge(ln_var, 2)
            link(newton(TMP[:, 3, :], ROOT, NEWT, NEWT))
            for j in range(CONF_TILES):
                dve.scalar_tensor_tensor(out=CA[:, j, :], in0=CA[:, j, :], scalar=col("ln_g", j), in1=NEWT,
                                         op0=ALU.mult, op1=ALU.mult).then_inc(ln_norm, 1)

            def la_triangle(m):
                g, t = divmod(m, 2)
                if m:
                    dve.wait_ge(d_done, m)
                    dve.wait_ge(e_done, m // 2)
                dve.tensor_tensor(LAT[:, :].rearrange("p (h l) -> p h l", h=HPG),
                                  LA[:, 32 * t + HPG * g:32 * t + HPG * (g + 1)].unsqueeze(2).to_broadcast([P, HPG, P]),
                                  TRI[:, :].unsqueeze(1).to_broadcast([P, HPG, P]), ALU.mult).then_inc(lat_ready, 1)

            def x_dt_end(g):
                if g:
                    dve.wait_ge(st_done, g)
                dve.tensor_tensor(XD2[:, :].rearrange("p (h c) -> p h c", h=HPG),
                                  XDT[:, 0, g * 512:(g + 1) * 512].rearrange("p (h c) -> p h c", h=HPG),
                                  DTE[:, HPG * g:HPG * (g + 1)].unsqueeze(2).to_broadcast([P, HPG, HP]),
                                  ALU.mult).then_inc(xd2_ready, 1)

            def cb_masked(m):
                dve.wait_ge(cb_done, m + 1)
                dve.tensor_tensor(CBM[:, :], bank[2][:, 0:P], TRI[:, :], ALU.mult).then_inc(cbm_ready, 1)
                dve.wait_ge(cbm_ready, m + 1)

            def heads_of(buf):
                return buf.rearrange("p (h l) -> p h l", h=HPG)

            def read_y(m):
                g, t = divmod(m, 2)
                dve.wait_ge(ssd_y, m + 1)
                for j in range(4):
                    xs = ZX[:, 4 * g + j, SEQ + t * P:SEQ + (t + 1) * P]
                    dve.scalar_tensor_tensor(out=xs, in0=xs, scalar=DSK[:, 4 * g + j:4 * g + j + 1],
                                             in1=bank[6 + t][:, j * P:(j + 1) * P], op0=ALU.mult, op1=ALU.add)\
                       .then_inc(y_read, 1)
                if t == 1:
                    dve.wait_ge(y_read, 4 * (m + 1))
                    y = ZX[:, 4 * g:4 * g + 4, SEQ:2 * SEQ]
                    dve.tensor_tensor(y, y, ZX[:, 4 * g:4 * g + 4, 0:SEQ], ALU.mult).then_inc(yz_ready, 1)

            la_triangle(0)
            dve.wait_ge(dte_ready, 1)
            dve.wait_ge(xdt_ready, 2 * GROUPS)
            x_dt_end(0)
            cb_masked(0)
            exps = 0
            for m in range(2 * GROUPS):
                g, t = divmod(m, 2)
                exps += 2
                dve.wait_ge(dec_ready, exps)
                dec = heads_of(DEC[:, m % 2, :])
                dve.tensor_tensor(dec, dec, CBM[:, :].unsqueeze(1).to_broadcast([P, HPG, P]), ALU.mult).then_inc(m_ready, 1)
                if m + 1 < 2 * GROUPS:
                    la_triangle(m + 1)
                    cb_masked(m + 1)
                if t == 1:
                    exps += 2
                    dve.wait_ge(dec_ready, exps)
                    ce = heads_of(CE[:, :])
                    dve.tensor_tensor(ce, ce, BC[:, 4 + g, P:2 * P].unsqueeze(1).to_broadcast([P, HPG, P]),
                                      ALU.mult).then_inc(ce_ready, 1)
                    if g + 1 < GROUPS:
                        x_dt_end(g + 1)
                if m:
                    read_y(m - 1)
            read_y(2 * GROUPS - 1)
            dve.wait_ge(ln_mean, 2)
            conf = Y[:, SSM_TILES:SSM_TILES + CONF_TILES, :]
            dve.tensor_tensor(conf[:, :, SEQ:2 * SEQ], CA[:, :, :], conf[:, :, 0:SEQ].bitcast(F32), ALU.subtract)\
               .then_inc(y_ready, 1)
            for k in range(2):
                dve.wait_ge(ynorm_sum, 2 * k + 2)
                dve.tensor_scalar(YV[:, 2 * k:2 * k + 2, :], bank[k][:, :].rearrange("p (g s) -> p g s", g=2),
                                  1.0 / (4 * P), EPS, ALU.mult, ALU.add).then_inc(dve_step, 1)
                steps[0] += 1
            dve.wait_ge(dve_step, steps[0])
            dve.tensor_copy(YT[:, 0, 0:1], YV[:, 0, 0:1]).then_inc(ynorm_var, 1)
            dve.wait_ge(ynorm_root, 1)
            link(newton(YV[:, :, :], YS[:, :, :], YT[:, :, :], YT[:, :, :]))
            for j in range(SSM_TILES):
                dve.scalar_tensor_tensor(out=YN[:, j, :], in0=ZX[:, j, SEQ:2 * SEQ], scalar=col("snorm", j),
                                         in1=YT[:, j // 4, :], op0=ALU.mult, op1=ALU.mult).then_inc(ynormed, 1)
            for g in range(GROUPS):
                dve.wait_ge(y_head, g + 1)
                y = Y[:, 4 * g:4 * g + 4, :]
                dve.tensor_tensor(y[:, :, SEQ:2 * SEQ], YN[:, 4 * g:4 * g + 4, :], y[:, :, 0:SEQ].bitcast(F32),
                                  ALU.subtract).then_inc(y_ready, 1)
            e = SPANS["out0"].unit
            for k in range(4, 10):
                tails(e, k, kt_at(e + k))

            def residual_group(t, halves, e, i, gain, uready, kts):
                for c in range(4):
                    dve.wait_ge(cols_done, e * 4 + c - 3)
                    h = H[:, ds(i * 4 + c, 1), :]
                    dve.tensor_tensor(h, bank[c][:, 0:SEQ].unsqueeze(1), h, ALU.add).then_inc(half_added, 1)
                    dve.wait_ge(half_added, halves + c + 1)
                    dve.tensor_tensor(h, bank[c][:, SEQ:2 * SEQ].unsqueeze(1), h, ALU.add).then_inc(bank_read, 1)
                for k, kt in enumerate(kts):
                    tails(e, k + 2, kt)
                    if k == 0 and gain is not None:
                        for c in range(4):
                            dve.wait_ge(u_head, uready + c + 1)
                            u = U[:, ds(i * 4 + c, 1), :]
                            dve.scalar_tensor_tensor(out=u[:, :, SEQ:2 * SEQ], in0=H[:, ds(i * 4 + c, 1), :],
                                                     scalar=dcol(gain[0], i * 4 + (c + gain[1])),
                                                     in1=u[:, :, 0:SEQ].bitcast(F32), op0=ALU.mult, op1=ALU.subtract)\
                               .then_inc(u_ready, 1)

            def residual_groups(name, n, gain, uready):
                s = SPANS[name]
                kts = ahead(s.unit + s.units, s.units, n)
                with dve.Fori(0, n) as i:
                    residual_group(i * 4 + s.tile, i * 4 + HALVES[name], i * s.units + (s.unit + s.units), i, gain,
                                   i * 4 + uready, kts)

            def out_projection(layer):
                name = f"out{layer}"
                s = SPANS[name]
                for i in range(s.groups):
                    e = s.unit + (i + 1) * s.units
                    residual_group(s.tile + 4 * i, HALVES[name] + 4 * i, e, i, ("ffn", layer * DT),
                                   (2 * layer + 1) * DT + 4 * i, ahead(e, 0, 1, range(2, 10 if i < 3 else 6)))
                variance(2 * layer + 2)
                norm_factor(2 * layer + 2)

            def mlp(layer):
                for b, (h0, n) in enumerate(CHUNKS):
                    s, gate0 = SPANS[f"up{layer}{b}"], layer * FT + h0
                    plain, conv = PLAIN[f"up{layer}{b}"], CONV[f"up{layer}{b}"]

                    def turn(i, turns):
                        for half in range(2):
                            first = s.unit + 4 * half + 4
                            kts = ahead(first + (8 * i if turns == 1 else 0), 8, turns)
                            e = i * 8 + first
                            read_banks(i * 8 + (plain + 4 * half), i * 8 + (s.tile + 4 * half), data)
                            tails(e, 2, kts[0])
                            for k, before, done in ((1, tap0, tap1_mlp), (2, tap1_mlp, taps_done)):
                                for c in range(4):
                                    t = i * 4 + (h0 + c + half * FT)
                                    base = conv if before is tap0 else conv - mlp_conv0(layer)
                                    dve.wait_ge(before, i * 8 + (base + 4 * half + c + 1))
                                    dve.scalar_tensor_tensor(out=ACC[:, c, :], in0=back(c, k),
                                                             scalar=dcol("fconv_w", t + (layer * 3 + 2 - k) * 2 * FT),
                                                             in1=ACC[:, c, :], op0=ALU.mult, op1=ALU.add).then_inc(done, 1)
                            if half == 1:
                                for c in range(4):
                                    dve.wait_ge(silu_done, i * 4 + (gate0 + c + 1))
                                    dve.wait_ge(taps_done, i * 8 + (conv + 4 + c + 1))
                                    dve.tensor_tensor(ACC[:, c, :], ACC[:, c, :], SG[:, c, :], ALU.mult).then_inc(gated, 1)
                            tails(e, 3, kts[1])
                            if half == 1:
                                for c in range(4):
                                    dve.wait_ge(hid_head, i * 4 + (gate0 + c + 1))
                                    y = Y[:, ds(i * 4 + c, 1), :]
                                    dve.tensor_tensor(y[:, :, SEQ:2 * SEQ], ACC[:, c:c + 1, :],
                                                      y[:, :, 0:SEQ].bitcast(F32), ALU.subtract).then_inc(hid_ready, 1)
                            tails(e, 4, kts[2])
                            tails(e, 5, kts[3])

                    turns = n // 4 - (b == len(CHUNKS) - 1)
                    with dve.Fori(0, turns) as i:
                        turn(i, turns)
                    if turns < n // 4:
                        turn(turns, 1)
                    name = f"down{layer}{b}"
                    if b < len(CHUNKS) - 1:
                        residual_groups(name, 4, None, 0)
                    else:
                        gain = ("mix", DT) if layer == 0 else None
                        residual_groups(name, 2, gain, 2 * DT)
                        s = SPANS[name]
                        for i in (2, 3):
                            e = s.unit + 4 * (i + 1)
                            residual_group(s.tile + 4 * i, HALVES[name] + 4 * i, e, i, gain, 2 * DT + 4 * i, rest(e))
                variance(2 * layer + 3)
                norm_factor(2 * layer + 3)

            out_projection(0)
            mlp(0)

            small_tails(2, NGATE)
            s = SPANS["in1"]
            kv_slot = {0: 8, 1: 12, 3: 16, 5: 20}
            conv, conv_base = 0, CONV["in1"]

            def rotate(c, dst):
                link(dve.tensor_tensor(SG[:, c, :], SG[:, c, :], SIN[:, :], ALU.mult))
                link(dve.tensor_tensor(ACC[:, c, :], data(c), COS[:, :], ALU.mult))
                dve.tensor_tensor(dst, ACC[:, c, :], SG[:, c, :], ALU.add).then_inc(kv_ready, 1)

            def blocks(i):
                if i:
                    dve.wait_ge(h1_done, i)
                for g in range(KVH):
                    toks = ZX[:, 8 + 4 * i + g, SEQ:2 * SEQ].rearrange("p (m r) -> p r m", r=CSTRIDE)
                    for a in range(CB // CSTRIDE):
                        l = slice(a * CSTRIDE, (a + 1) * CSTRIDE)
                        c0 = PARAMS["pe"][0] + i * CB + a * CSTRIDE
                        dve.tensor_tensor(BLK[:, l, g * NCMP:(g + 1) * NCMP], toks[:, :, a:a + NCMP],
                                          PAR[:, c0:c0 + CSTRIDE].unsqueeze(2).to_broadcast([P, CSTRIDE, NCMP]),
                                          ALU.add).then_inc(blk_ready, 1)

            ropes = 0
            for q in range(s.groups):
                e, last = s.unit + 4 * (q + 1), q == s.groups - 1
                if q in kv_slot:
                    dst = lambda c: ZX[:, kv_slot[q] + c, SEQ:2 * SEQ]
                elif q in (10, 11):
                    dst = lambda c: CA[:, 4 * (q - 10) + c, :]
                else:
                    dst = data
                read_banks(PLAIN["in1"] + 4 * q, s.tile + 4 * q, dst)
                kts = ahead(e, 0, 1)
                tails(e, 2, kts[0])
                if q in (2, 4, 6, 7, 8, 9):
                    for c in range(4):
                        ropes += 2
                        dve.wait_ge(swap_ready, ropes)
                        if q == 2:
                            rotate(c, BC[:, 2 * c, :])
                        elif q == 4:
                            rotate(c, BC[:, 2 * c + 1, :])
                        else:
                            rotate(c, ZX[:, 8 + 4 * (q - 6) + c, 0:SEQ])
                if q in (12, 13):
                    for c in range(4):
                        j = 4 * (q - 12) + c
                        dve.wait_ge(scaled, PLAIN["in1"] + 4 * q + c + 1)
                        dve.tensor_tensor(data(c), data(c), CA[:, j, :], ALU.mult).then_inc(conv_in, 1)
                    for k, before, done in ((1, tap0, tap1), (2, tap1, taps_done)):
                        for c in range(4):
                            j = 4 * (q - 12) + c
                            dve.wait_ge(before, (conv_base if k == 1 else 4 * EVEN_XBC_GROUPS) + j + 1)
                            dve.scalar_tensor_tensor(out=ACC[:, c, :] if k == 1 else CA[:, j, :], in0=back(c, k),
                                                     scalar=col("sc_w", (2 - k) * 8 + j), in1=ACC[:, c, :],
                                                     op0=ALU.mult, op1=ALU.add).then_inc(done, 1)
                if q in (14, 15):
                    for c in range(4):
                        j = 4 * (q - 14) + c
                        dve.wait_ge(taps_done, conv_base + j + 1)
                        dve.wait_ge(scaled, PLAIN["in1"] + 4 * q + c + 1)
                        dve.tensor_tensor(ACC[:, c, :], data(c), CA[:, j, :], ALU.mult).then_inc(yc_ready, 1)
                tails(e, 3, kts[1])
                if q in (14, 15):
                    dve.wait_ge(yc_head, q - 13)
                    y = Y[:, 4 * (q - 14):4 * (q - 14) + 4, :]
                    dve.tensor_tensor(y[:, :, SEQ:2 * SEQ], ACC[:, :, :], y[:, :, 0:SEQ].bitcast(F32), ALU.subtract)\
                       .then_inc(y_ready, 1)
                if q == 1:
                    small_scaled(2, NGATE, GT)
                    dve.tensor_copy(RTOK, RTOK).then_inc(gates_in, 1)
                if q == COMPRESS[0] - 1:
                    blocks(0)
                if q == COMPRESS[0] + 1:
                    blocks(1)
                if q == COMPRESS[1] + 1:
                    dve.wait_ge(kc_ready, 3)

                    def at_ends(table):
                        return table[:, CB - 1:SEQ:CSTRIDE].unsqueeze(1).to_broadcast([P, KVH, NCMP])

                    def by_head(a):
                        return a.rearrange("p (g n) -> p g n", g=KVH)

                    link(dve.tensor_tensor(by_head(KSW), by_head(KSW), at_ends(SIN), ALU.mult))
                    link(dve.tensor_tensor(by_head(KCR), by_head(KC0), at_ends(COS), ALU.mult))
                    link(dve.tensor_tensor(KCR, KCR, KSW, ALU.add))
                    dve.tensor_copy(KC0, KC0).then_inc(kv_ready, 1)
                if not last:
                    tails(e, 4, kts[2])
                    tails(e, 5, kts[3])

            dve.wait_ge(gates_ready, 1)
            dve.wait_ge(mask_ready, 1)
            items = NSA_HEADS * NT

            def branches(a, nk):
                return a.rearrange("p (r k) -> p r k", r=2)[:, :, 0:nk]

            for n in range(items + 4):
                if n < items:
                    b, t = n % 2, n % NT
                    nk = P * (t + 1)
                    p3 = PROB[:, n % 3, :]
                    if n >= 3:
                        dve.wait_ge(pt_done, n - 2)
                    dve.wait_ge(s_done, n + 1)
                    dve.tensor_tensor(p3[:, 512:512 + NCMP], bank[2 + b][:, 0:NCMP], CMPM[:, t, :], ALU.add)
                    dve.tensor_tensor(branches(p3[:, 0:512], nk), branches(bank[b][:, :], nk),
                                      MASK[:, 2 * P - nk:2 * P].unsqueeze(1).to_broadcast([P, 2, nk]), ALU.add)\
                       .then_inc(s_read, 1)
                    dve.wait_ge(s_read, n + 1)
                    dve.tensor_reduce(MX[:, 4 * b:4 * b + 1], p3[:, 512:512 + NCMP], AXX, ALU.max)
                    link(dve.tensor_reduce(MX[:, 4 * b + 1:4 * b + 3], branches(p3[:, 0:512], nk), AXX, ALU.max))
                    dve.tensor_scalar(MX[:, 4 * b:4 * b + 3], MX[:, 4 * b:4 * b + 3], -SCALE, -NEG * 1e-6,
                                      ALU.mult, ALU.min).then_inc(mx_ready, 1)
                if 1 <= n <= items:
                    m = n - 1
                    b, (h, t) = m % 2, divmod(m, NT)
                    nk = P * (t + 1)
                    dve.wait_ge(p_ready, 3 * (m + 1))
                    f = FAC[:, 4 * b:4 * b + 3]
                    if t == 0:
                        link(dve.tensor_scalar(SUMS[:, 4 * b:4 * b + 1], SUMS[:, 4 * b:4 * b + 1], 0.5, None, ALU.max))
                    link(dve.reciprocal(f, SUMS[:, 4 * b:4 * b + 3]))
                    link(dve.tensor_tensor(f, f, GT[:, t * NGATE + 3 * h:t * NGATE + 3 * h + 3], ALU.mult))
                    for r in range(2):
                        pr = PROB[:, m % 3, r * SEQ:r * SEQ + nk]
                        dve.tensor_scalar(pr, pr, FAC[:, 4 * b + 1 + r:4 * b + 2 + r], None, ALU.mult).then_inc(pn_ready, 1)
                    pr = PROB[:, m % 3, 512:512 + NCMP]
                    dve.scalar_tensor_tensor(out=pr, in0=pr, scalar=FAC[:, 4 * b:4 * b + 1], in1=CMP1[:, t, :],
                                             op0=ALU.mult, op1=ALU.mult).then_inc(pn_ready, 1)
                if n >= 4:
                    m = n - 4
                    h, t = divmod(m, NT)
                    dve.wait_ge(o_head, m + 1)
                    y = Y[:, 8 + h, :]
                    dve.tensor_tensor(y[:, SEQ + t * P:SEQ + (t + 1) * P], bank[6 + m % 2][:, 0:P],
                                      y[:, t * P:(t + 1) * P].bitcast(F32), ALU.subtract).then_inc(y_ready, 1)
            e = SPANS["out1"].unit
            for k in range(4, 10):
                tails(e, k, kt_at(e + k))
            out_projection(1)
            mlp(1)

            for j in range(DT):
                dve.scalar_tensor_tensor(out=H[:, j, :], in0=H[:, j, :], scalar=col("final", j), in1=RSTD[:, :],
                                         op0=ALU.mult, op1=ALU.mult).then_inc(out_scaled, 1)
            for k in range(0, 4 * NT, 2):
                dve.wait_ge(out_turned, k + 1)
                dve.tensor_copy(OST[:, k // 4, (k % 4) * 512:(k % 4 + 1) * 512], bank[4 + k % 4][:, :])\
                   .then_inc(out_read, 1)

        @block.tensor
        def _(pe):
            def product_group(unit, tile, s, rhs, ready=None, first=False, after=None):
                for u in range(s.units):
                    pe.wait_ge(tails_ready, unit + (u + 1))
                    if ready is not None:
                        pe.wait_ge(ready[0], ready[1] + (u + 1) * s.kt if ready[2] else ready[1])
                    for c in range(4):
                        if u == 0 and not first:
                            pe.wait_ge(bank_read, tile + (c - 3))
                        for k in range(s.kt):
                            cols = slice(k * CW + c * P, k * CW + (c + 1) * P)
                            head, tail = WHEAD[:, u % RING, cols], WTAIL[:, u % RING, cols]
                            both, one = rhs[:, u * s.kt + k, :], rhs[:, u * s.kt + k, 0:SEQ]
                            begin, end = u == 0 and k == 0, u == s.units - 1 and k == s.kt - 1
                            if begin:
                                pe.matmul(bank[c][:, :], head, both, start=True, stop=False)
                                mm = pe.matmul(bank[c][:, 0:SEQ], tail, one, start=False, stop=False)
                            else:
                                pe.matmul(bank[c][:, 0:SEQ], tail, one, start=False, stop=False)
                                mm = pe.matmul(bank[c][:, :], head, both, start=False, stop=end)
                        mm.then_inc(cols_done, 1)
                    if after and u == 1:
                        after()

            def product(name, rhs, ready=None, begin=0, end=None, after=None):
                s = SPANS[name]
                end = s.groups if end is None else end
                if begin == 0:
                    product_group(s.unit, s.tile, s, rhs, ready, first=s.tile == 0, after=after)
                    begin = 1
                if end > begin:
                    with pe.Fori(begin, end) as i:
                        product_group(i * s.units + s.unit, i * 4 + s.tile, s, rhs)

            def sum_statistics(n):
                def go():
                    pe.wait_ge(stat_added, DT * n)
                    pe.matmul(bank[4][:, 0:SEQ], ONES[:, :], STAT[:, :], start=True, stop=True).then_inc(stat_summed, 1)
                return go

            def small_product(count, n):
                pe.wait_ge(ws_ready, count)
                pe.wait_ge(var_ready, 2 * count - 1)
                for t in range(NT):
                    for k in range(DT):
                        uh = U[:, k, t * P:(t + 1) * P]
                        ut = U[:, k, SEQ + t * P:SEQ + (t + 1) * P]
                        dst = bank[4][:, 64 * t:64 * t + n]
                        pe.matmul(dst, ut, WS_HEAD[:, k, 0:n], start=k == 0, stop=False)
                        pe.matmul(dst, uh, WS_TAIL[:, k, 0:n], start=False, stop=False)
                        pe.matmul(dst, uh, WS_HEAD[:, k, 0:n], start=False, stop=k == DT - 1)
                pe.wait_ge(rstd_ready, 2 * count - 1)
                for t in range(NT):
                    tr = pe.transpose(bank[5][:, t * P:(t + 1) * P], RSTD[:, t * P:(t + 1) * P], IDENT[:, :])
                tr.then_inc(rtok_turned, 1)

            pe.wait_ge(consts, CONSTS)
            pe.wait_ge(par_landed, 16 * PAR_LOADS)
            for b in range(-(-PTILES // 4)):
                for tile in range(4 * b, min(4 * b + 4, PTILES)):
                    r = min(P, NPARAM - tile * P)
                    tr = pe.transpose(bank[b][:, (tile % 4) * P:(tile % 4) * P + r], PST[0:r, tile, :], IDENT[0:r, 0:r])
                tr.then_inc(pturned, 1)
            pe.wait_ge(x_landed, 16 * NT)
            for k in range(8):
                if k >= 4:
                    pe.wait_ge(turned_read, k - 3)
                for j in range(2):
                    for t in range(NT):
                        tr = pe.transpose(bank[4 + k % 4][:, (2 * j + t) * P:(2 * j + t + 1) * P],
                                          XST[:, t, (2 * k + j) * P:(2 * k + j + 1) * P], IDENT[:, :])
                tr.then_inc(turned, 1)
            pe.wait_ge(pturned_read, -(-PTILES // 4))
            pe.wait_ge(turned_read, 8)

            product("in0", U, (u_ready, 0, True), 0, 1, after=sum_statistics(1))
            small_product(1, HEADS)
            product("in0", U, None, 1)

            pe.wait_ge(conf_dve, (CONF_TILES - POOL_CONF) * (CONF_TAPS - 1))
            pe.wait_ge(conf_pool, POOL_CONF)
            pe.wait_ge(bank_read, SPANS["in0"].tile_end)
            for j in range(CONF_TILES):
                mm = pe.matmul(bank[0][:, 0:SEQ], ONES[:, :], CA[:, j, :], start=j == 0, stop=j == CONF_TILES - 1)
            mm.then_inc(ln_sum, 1)
            pe.wait_ge(x_ready, 24)
            for g in range(GROUPS):
                tr = pe.transpose(bank[2][:, g * P:(g + 1) * P], BC[:, g, 0:P], IDENT[:, :])
            tr.then_inc(bt_turned, 1)
            pe.wait_ge(la_ready, NT)
            pe.matmul(bank[3][:, 0:HEADS], UST[:, :], LA[:, 0:HEADS], start=True, stop=True).then_inc(dte_sum, 1)
            for k in range(2 * GROUPS):
                g, t = divmod(k, 2)
                if k >= 4:
                    pe.wait_ge(xdt_ready, k - 3)
                for j in range(4):
                    tr = pe.transpose(bank[4 + k % 4][:, j * P:(j + 1) * P],
                                      ZX[:, 4 * g + j, SEQ + t * P:SEQ + (t + 1) * P], IDENT[:, :])
                tr.then_inc(xt_turned, 1)
            pe.wait_ge(ln_sq, 1)
            for j in range(CONF_TILES):
                mm = pe.matmul(bank[1][:, 0:SEQ], ONES[:, :], CP[:, j, 0:SEQ], start=j == 0, stop=j == CONF_TILES - 1)
            mm.then_inc(ln_sum, 1)

            def decays(m):
                g, t = divmod(m, 2)
                pe.wait_ge(lat_ready, m + 1)
                if m == 0:
                    pe.wait_ge(xdt_ready, 2 * GROUPS)
                else:
                    pe.wait_ge(dec_ready, EXPS[m - 1])
                for h in range(2):
                    mm = pe.matmul(bank[4 + h][:, :], UST[:, :], LAT[:, h * 512:(h + 1) * 512], start=True, stop=True)
                mm.then_inc(d_done, 1)
                if m == 0:
                    pe.wait_ge(btok_ready, 1)
                else:
                    pe.wait_ge(cbm_ready, m)
                c = slice(t * P, (t + 1) * P)
                pe.matmul(bank[2][:, 0:P], BC[:, g, c], BC[:, 4 + g, c], start=True, stop=True).then_inc(cb_done, 1)
                if t == 0:
                    pe.wait_ge(xd2_ready, g + 1)
                    pe.matmul(bank[3][:, :], BTOK[:, g, :], XD2[:, :], start=True, stop=True).then_inc(st_done, 1)
                else:
                    if g == 0:
                        pe.wait_ge(ln_var, 1)
                    for h in range(2):
                        mm = pe.matmul(bank[h][:, :], ONES[:, :], LAT[:, h * 512:(h + 1) * 512], start=True, stop=True)
                    mm.then_inc(e_done, 1)

            pe.wait_ge(dte_ready, 1)
            decays(0)
            for m in range(2 * GROUPS):
                g, t = divmod(m, 2)
                if m + 1 < 2 * GROUPS:
                    decays(m + 1)
                pe.wait_ge(m_ready, m + 1)
                if m >= 2:
                    pe.wait_ge(y_read, 4 * (m - 1))
                if t == 1:
                    pe.wait_ge(ce_ready, g + 1)
                    pe.wait_ge(st_ready, g + 1)
                for h in range(HPG):
                    rows, hc = slice(HP * (h % 2), HP * (h % 2) + HP), slice(h * P, (h + 1) * P)
                    dst = bank[6 + t][rows, (h // 2) * P:(h // 2 + 1) * P]
                    x_h = XDT[:, t, (HPG * g + h) * HP:(HPG * g + h + 1) * HP]
                    mm = pe.matmul(dst, x_h, DEC[:, m % 2, hc], start=True, stop=t == 0)
                    if t == 1:
                        mm = pe.matmul(dst, ST[:, h * HP:(h + 1) * HP], CE[:, hc], start=False, stop=True)
                mm.then_inc(ssd_y, 1)
            for g in range(GROUPS):
                pe.wait_ge(ysq_ready, g + 1)
                pe.matmul(bank[g // 2][:, (g % 2) * SEQ:(g % 2 + 1) * SEQ], ONES[:, :], ZX[:, 4 * g, 0:SEQ],
                          start=True, stop=True).then_inc(ynorm_sum, 1)
            product("out0", Y, (y_ready, 5, False))

            def mlp(layer):
                for b, (h0, n) in enumerate(CHUNKS):
                    product(f"up{layer}{b}", U, (u_ready, (2 * layer + 1) * DT, True) if b == 0 else None,
                            after=sum_statistics(2 * layer + 2) if b == 0 else None)
                    product(f"down{layer}{b}", Y, (hid_ready, layer * FT + h0, True))

            mlp(0)
            product("in1", U, (u_ready, 2 * DT, True), 0, 1, after=sum_statistics(3))
            small_product(2, NGATE)
            def compress(i):
                pe.wait_ge(w1_landed, 16 * (i + 1))
                pe.wait_ge(blk_ready, 8 * (i + 1))
                for l in range(CB):
                    mm = pe.matmul(bank[4][:, 0:KVH * NCMP], W1[:, l, :], BLK[:, l, :], start=l == 0, stop=l == CB - 1)
                mm.then_inc(h1_done, 1)

            product("in1", U, None, 1, COMPRESS[0] + 1)
            compress(0)
            product("in1", U, None, COMPRESS[0] + 1, COMPRESS[1] + 1)
            pe.wait_ge(w2_landed, 16)
            pe.wait_ge(s1_ready, 1)
            pe.matmul(bank[5][:, 0:KVH * NCMP], W2[:, 0:P], S1K, start=True, stop=True).then_inc(kc_done, 1)
            compress(1)
            product("in1", U, None, COMPRESS[1] + 1, COMPRESS[2] + 1)
            pe.wait_ge(s1_ready, 2)
            pe.wait_ge(kc_ready, 3)
            for g in range(KVH):
                mm = pe.matmul(bank[5][0:NCMP, g * HD:(g + 1) * HD], S1K[:, g * NCMP:(g + 1) * NCMP],
                               W2[:, P:2 * P], start=True, stop=True)
            mm.then_inc(kc_done, 1)
            product("in1", U, None, COMPRESS[2] + 1, SPANS["in1"].groups - 1)
            pe.wait_ge(vc_ready, 1)
            for k in range(4):
                for g in range(KVH):
                    tr = pe.transpose(bank[4 + k][:, g * P:(g + 1) * P],
                                      ZX[:, 16 + 4 * (k // 2) + g, SEQ + (k % 2) * P:SEQ + (k % 2 + 1) * P], IDENT[:, :])
                tr.then_inc(vt_turned, 1)
            product("in1", U, None, SPANS["in1"].groups - 1)

            pe.wait_ge(kv_ready, 4 * 6 + 1)
            pe.wait_ge(bank_read, SPANS["in1"].tile_end)
            pe.wait_ge(vt_ready, 4)
            items = NSA_HEADS * NT
            for n in range(items + 3):
                if n < items:
                    b, (h, t) = n % 2, divmod(n, NT)
                    g = h // (NSA_HEADS // KVH)
                    if n >= 2:
                        pe.wait_ge(s_read, n - 1)
                    if n >= 3:
                        pe.wait_ge(pt_read, 2 * (n - 2))
                    qh = ZX[:, 8 + h, t * P:(t + 1) * P]
                    if t == NT - 1:
                        pe.matmul(bank[b][:, :], qh, BC[:, 2 * g:2 * g + 2, :], start=True, stop=True)
                    else:
                        for r in range(2):
                            pe.matmul(bank[b][:, r * SEQ:r * SEQ + P], qh, BC[:, 2 * g + r, 0:P], start=True, stop=True)
                    pe.matmul(bank[2 + b][:, 0:NCMP], qh, KCR[:, g * NCMP:(g + 1) * NCMP], start=True, stop=True)\
                      .then_inc(s_done, 1)
                if 2 <= n < items + 2:
                    m = n - 2
                    b, t = m % 2, m % NT
                    pe.wait_ge(pn_ready, 3 * (m + 1))
                    pe.wait_ge(s_read, min(m + 2, items))
                    if m >= 2:
                        pe.wait_ge(pt_read, 2 * (m - 1))
                    i = 0
                    for r in range(2):
                        for kb in range(t + 1):
                            pe.transpose(bank[4 + b][:, i * P:(i + 1) * P],
                                         PROB[:, m % 3, r * SEQ + kb * P:r * SEQ + (kb + 1) * P], IDENT[:, :])
                            i += 1
                    pe.transpose(bank[3 - b][0:NCMP, P:2 * P], PROB[:, m % 3, 512:512 + NCMP], IDENT[:, :]).then_inc(pt_done, 1)
                if n >= 3:
                    m = n - 3
                    b, (h, t) = m % 2, divmod(m, NT)
                    g = h // (NSA_HEADS // KVH)
                    pe.wait_ge(pt_read, 2 * (m + 1))
                    if m >= 2:
                        pe.wait_ge(y_ready, 5 + 2 + m - 1)
                    i = 0
                    for r in range(2):
                        for kb in range(t + 1):
                            pe.matmul(bank[6 + b][:, 0:P], VTOK[:, kb, 4 * r + g, :], PT[:, b, i * P:(i + 1) * P],
                                      start=i == 0, stop=False)
                            i += 1
                    pe.matmul(bank[6 + b][:, 0:P], VCT[:, g * HD:(g + 1) * HD], PTC[0:NCMP, b, :], start=False, stop=True)\
                      .then_inc(o_done, 1)
            product("out1", Y, (y_ready, 5 + 2 + items, False))
            mlp(1)
            sum_statistics(5)()
            for k in range(4 * NT):
                t, b = divmod(k, 4)
                pe.wait_ge(out_scaled, 4 * (b + 1) if t == 0 else DT)
                if k == 0:
                    pe.wait_ge(var_ready, 5)
                if k >= 4:
                    pe.wait_ge(out_read if k % 2 == 0 else store_ready, (k - 4) // 2 + 1)
                for i in range(4):
                    tr = pe.transpose(bank[4 + k % 4][:, i * P:(i + 1) * P], H[:, 4 * b + i, t * P:(t + 1) * P], IDENT[:, :])
                tr.then_inc(out_turned, 1)


_INS = ["x", "positions", "inv_freq", "mix_norm", "ffn_norm", "final_norm", "ab_w_in", "ssm_conv_w", "ssm_conv_b",
        "ssm_dt_bias", "ssm_a_log", "ssm_d", "ssm_norm", "conf_dw_w", "conf_dw_b", "conf_ln_g", "conf_ln_b",
        "ab_w_out", "cd_w_in", "sc_conv_w", "nsa_cmp_pe", "nsa_cmp_w1", "nsa_cmp_w2", "cd_w_out",
        "ffn_w_up", "ffn_conv_w", "ffn_conv_b", "ffn_w_down"]


def kernel(**inputs):
    import numpy as _np
    import concourse.bacc as _bacc
    from concourse import mybir as _mybir
    from concourse.bass_utils import run_bass_kernel_spmd as _run

    nc = _bacc.Bacc("TRN2", target_bir_lowering=False, num_devices=1)
    half = HD // 2
    inv = _np.float32(10000.0) ** (-_np.arange(half, dtype=_np.float32) / _np.float32(half))
    constants = {"inv_freq": _np.tile(inv.astype(_np.float32), 2).reshape(P, 1)}
    arrays, args = {}, []
    for name in _INS:
        a = _np.ascontiguousarray(constants[name] if name in constants else inputs[name])
        arrays[f"in_{name}"] = a
        args.append(nc.dram_tensor(f"in_{name}", a.shape, _mybir.dt.from_np(a.dtype), kind="ExternalInput").ap())
    args.append(nc.dram_tensor("out_0", (1, SEQ, D), F32, kind="ExternalOutput").ap())
    build(nc, *args)
    r = _run(nc, [arrays], core_ids=[0])
    return r.results[0]["out_0"]
```

```python
from contextlib import ExitStack

import numpy as np
import concourse.bass as bass
from concourse import mybir

F32 = mybir.dt.float32
F32R = mybir.dt.float32r
I32 = mybir.dt.int32
ACT = mybir.ActivationFunctionType
ALU = mybir.AluOpType
AXX = mybir.AxisListType.X
ds = bass.ds

P = 128
D = 2048
SEQ = 256
NT = SEQ // P
DT = D // P
EPS = 1e-6
ARENA = 53152
CW = 512
RING = 4
UNIT = 4 * CW

HEADS, GROUPS, HP, STATE = 32, 4, 64, 128
HPG = HEADS // GROUPS
SSM_TILES = D // P
CONF_TILES = 8
CONF_TAPS = 31
POOL_CONF = 4
CONV_DIM = D + 2 * GROUPS * STATE
ZC, XBCC, DTC, GLUC = 0, D, D + CONV_DIM, D + CONV_DIM + HEADS
NSA_HEADS, KVH, HD = 16, 4, 128
SC = 1024
QC, KVC, GATEC = 3 * SC, 3 * SC + D, 3 * SC + D + 6 * KVH * HD
NGATE = 3 * NSA_HEADS
CB, CSTRIDE = 32, 16
NCMP = (SEQ - CB) // CSTRIDE + 1
SCALE = float(HD) ** -0.5
NEG = -1e30
FT = 44
FF = FT * P
CHUNKS = [(0, 16), (16, 16), (32, 12)]


class Span:

    def __init__(self, unit, tile, groups, units, kt):
        self.unit, self.tile, self.groups, self.units, self.kt = unit, tile, groups, units, kt
        self.unit_end, self.tile_end = unit + groups * units, tile + 4 * groups


def mlp_conv0(layer):
    return 4 * EVEN_XBC_GROUPS + (SC // P if layer else 0)


def plan():
    spans, unit, tile = {}, 0, 0

    def add(name, groups, units, kt):
        nonlocal unit, tile
        spans[name] = Span(unit, tile, groups, units, kt)
        unit, tile = spans[name].unit_end, spans[name].tile_end

    for layer in range(2):
        add(f"in{layer}", (14, 16)[layer], 4, 4)
        add(f"out{layer}", 4, 8, 3)
        for b, (_, n) in enumerate(CHUNKS):
            add(f"up{layer}{b}", n // 2, 4, 4)
            add(f"down{layer}{b}", 4, 4, n // 4)
    return spans


SPANS = plan()


def kt_at(unit):
    return next((s.kt for s in SPANS.values() if s.unit <= unit < s.unit_end), 4)


def ahead(e, step, n, offsets=(2, 3, 4, 5)):
    kts = [kt_at(e + k) for k in offsets]
    assert all([kt_at(e + k + i * step) for k in offsets] == kts for i in range(n)), (e, step, n)
    return kts


LAST_UNIT = max(s.unit_end for s in SPANS.values())


def rest(e):
    return [kt_at(u) for u in range(e + 2, e + 6) if u < LAST_UNIT]


PLAIN = {}
_n = 0
for _name, _s in SPANS.items():
    if _name[:2] in ("in", "up"):
        PLAIN[_name] = _n
        _n += 4 * _s.groups
EVEN_XBC_GROUPS = 6
CONV = {"in0": 0}
_n = 4 * EVEN_XBC_GROUPS
for _l in range(2):
    if _l == 1:
        CONV["in1"] = _n
        _n += SC // P
    for _b, (_, _c) in enumerate(CHUNKS):
        CONV[f"up{_l}{_b}"] = _n
        _n += 2 * _c

HALVES = {}
_n = 0
for _name, _s in SPANS.items():
    if _name not in PLAIN:
        HALVES[_name] = _n
        _n += 4 * _s.groups
COMPRESS = (3, 5, 7)
LAST_SQUARES = 2
CONSTS = 8
EXPS = [2 * (m + 1) + 2 * (m // 2) for m in range(2 * GROUPS)]
ROUNDER = float(1.5 * 2 ** 23)
PI = 3.1415925


def _turn_parts():
    first = 6.28125
    second = float(np.float32(np.floor((2 * np.pi - first) * 2 ** 20) / 2 ** 20))
    return first, second, float(np.float32(2 * np.pi - first - second))


TURN = _turn_parts()


PARAMS = {}
_c = 0
for _name, _r in (("mix", 32), ("ffn", 32), ("final", 16), ("sconv_w", 96), ("sconv_b", 24),
                  ("snorm", 16), ("dw_w", 248), ("dw_b", 8), ("ln_g", 8), ("ln_b", 8),
                  ("sc_w", 24), ("pe", 64), ("fconv_w", 528), ("fconv_b", 176)):
    PARAMS[_name] = (_c, _r)
    _c += _r
NPARAM = _c
PTILES = -(-NPARAM // P)
PBANKS = -(-(PTILES - 1) // 4)
PAR_FIRST = sum(c < P for c, _ in PARAMS.values())
PAR_LOADS = sum((c + n - 1) // P - c // P + 1 for c, n in PARAMS.values())


def build(nc, x, positions, inv_freq, mix_norm, ffn_norm, final_norm, ab_w_in, ssm_conv_w, ssm_conv_b,
          ssm_dt_bias, ssm_a_log, ssm_d, ssm_norm, conf_dw_w, conf_dw_b, conf_ln_g, conf_ln_b,
          ab_w_out, cd_w_in, sc_conv_w, nsa_cmp_pe, nsa_cmp_w1, nsa_cmp_w2, cd_w_out,
          ffn_w_up, ffn_conv_w, ffn_conv_b, ffn_w_down, out):
    stack = ExitStack()
    with stack:
        base = (nc.sbuf_base + 31) // 32 * 32
        stack.enter_context(nc.sbuf_tensor("arena", [P, ARENA], F32))
        used = [0]

        def at(name, offset, shape, dtype):
            return nc.alloc_sbuf_tensor_at(name, shape, dtype, offset=base + offset)

        def take(name, shape, dtype):
            size = 4 * int(np.prod(shape[1:]))
            t = at(name, used[0], shape, dtype)
            places[name] = used[0]
            used[0] += (size + 31) // 32 * 32
            assert used[0] <= ARENA * 4, (name, used[0])
            return t

        places = {}
        H = take("residual", [P, DT, SEQ], F32)
        WTAIL = take("weight_tail", [P, RING, UNIT], F32R)
        WRAW = at("weight_raw", places["weight_tail"], [P, RING, UNIT], F32)
        WHEAD = take("weight_head", [P, RING, UNIT], F32R)
        U = take("norm_in", [P, DT, 2 * SEQ], F32R)
        Y = take("mixed", [P, 24, 2 * SEQ], F32R)
        TMP = take("half", [P, 4, SEQ], F32)
        YP = take("padded", [P, 4, SEQ + 4], F32)
        ACC = take("conv_acc", [P, 4, SEQ], F32)
        SG = take("gate", [P, 4, SEQ], F32)
        BC = take("bc", [P, 8, SEQ], F32)
        CA = take("ca", [P, 8, SEQ], F32)
        PAR = take("params", [P, PTILES * P], F32)
        IDENT = take("ident", [P, P], F32)
        ONES = take("ones", [P, P], F32)
        TRI = take("tri", [P, P], F32)
        UST = take("ust", [P, P], F32)
        MASK = at("causal", places["tri"], [P, 2 * P], F32)
        RSTD = take("rstd", [P, SEQ], F32)
        STAT = take("stat", [P, SEQ], F32)
        SQ = take("squares", [P, SEQ], F32)
        COS = take("cos", [P, SEQ], F32)
        SIN = take("sin", [P, SEQ], F32)
        CMPM = take("cmp_mask", [P, NT, NCMP], F32)
        CMP1 = take("cmp_keep", [P, NT, NCMP], F32)
        SMALL = take("small", [P, 672], F32)

        ZX = at("zx", places["mixed"], [P, 24, 2 * SEQ], F32)
        XST = at("x_stage", places["mixed"], [P, NT, D], F32)
        PST = at("param_stage", places["mixed"] + 16384, [P, PTILES, P], F32)
        CP = at("conf_pad", places["mixed"] + 16 * 2048, [P, 8, 2 * SEQ], F32)
        WS_RAW = at("ws_raw", places["bc"], [P, DT, NGATE], F32)
        WS_TAIL = at("ws_tail", places["bc"], [P, DT, NGATE], F32R)
        WS_HEAD = at("ws_head", places["bc"] + 4 * DT * NGATE, [P, DT, NGATE], F32R)
        XDT = at("x_dt", places["norm_in"], [P, NT, D], F32)
        LAT = at("la_tri", places["norm_in"] + 16384, [P, HPG * P], F32)
        DEC = at("decay", places["norm_in"] + 20480, [P, 2, HPG * P], F32)
        CE = at("c_exp", places["norm_in"] + 28672, [P, HPG * P], F32)
        VTOK = at("v_tok", places["norm_in"], [P, NT, 8, HD], F32)
        PROB = at("prob", places["norm_in"] + 8192, [P, 3, 528], F32)
        PT = at("prob_t", places["norm_in"] + 16384, [P, 2, 512], F32)
        PTC = at("prob_tc", places["norm_in"] + 20480, [P, 2, P], F32)
        W1 = at("w1", places["mixed"], [P, CB, HD], F32)
        BLK = at("blk", places["ca"], [P, CB, KVH * NCMP], F32)
        HG = at("h_gained", places["norm_in"], [P, DT, SEQ], F32)
        OST = at("out_stage", places["norm_in"] + 16384, [P, NT, D], F32)
        LATS = (LAT, at("la_tri2", places["gate"], [P, HPG * P], F32))
        ROOT, NEWT = TMP[:, 0, :], TMP[:, 1, :]
        LNR, LNF, LNM = SG[:, 0, :], SG[:, 1, :], SG[:, 3, :]
        DTB, ALG = SMALL[:, 0:32], SMALL[:, 32:64]
        AN = SMALL[:, 64:96]
        DSK = SMALL[:, 96:112]
        DTV = SMALL[:, 112:176]
        LA = SMALL[:, 176:240]
        DTE = SMALL[:, 240:272]
        S1, S2, S3, S4 = (SMALL[:, 272 + 64 * i:336 + 64 * i] for i in range(4))
        RTOK = SMALL[:, 528:530]
        RVAR, RSQ, RNEW = SMALL[:, 530:532], SMALL[:, 532:534], SMALL[:, 534:536]
        INV = SMALL[:, 640:641]
        YV, YS, YT = SQ, TMP[:, 3, :], STAT
        BTOK = at("b_tok", places["conv_acc"], [P, GROUPS, STATE], F32)
        ST = at("state", places["conv_acc"] + 2048, [P, HPG * HP], F32)
        XD2 = at("x_dt_end", places["half"], [P, HPG * HP], F32)
        CBM = at("cb_masked", places["half"] + 2048, [P, 2, P], F32)
        DALL = SMALL[:, 112:144]
        POSI = at("pos_i", places["small"] + 4 * 384, [P, SEQ], I32)
        GT = SMALL[:, 0:96]
        MX, SUMS, FAC = SMALL[:, 96:104], SMALL[:, 104:112], SMALL[:, 112:120]
        KCR = SMALL[:, 128:188]
        S1K, KSW, KC0 = SMALL[:, 192:252], SMALL[:, 256:316], SMALL[:, 320:380]
        W2 = SQ[:, :]
        VCT = SG[0:NCMP, 2:4, :].rearrange("p a b -> p (a b)")

        bank = [stack.enter_context(nc.psum_tensor(f"bank{i}", [P, 512], F32)) for i in range(8)]

        def sem(name):
            return stack.enter_context(nc.semaphore(name))

        x_landed, par_first, par_landed, misc_landed = (
            sem(n) for n in ("x_landed", "par_first", "par_landed", "misc_landed"))
        raw_landed = [sem(f"raw_landed{i}") for i in range(RING)]
        ws_landed, w1_landed, w2_landed = sem("ws_landed"), sem("w1_landed"), sem("w2_landed")
        stored = sem("stored")
        heads_ready = sem("heads_ready")
        tails_ready = sem("tails_ready")
        cols_done = sem("cols_done")
        half_copied = sem("half_copied")
        bank_read = sem("bank_read")
        scaled = sem("scaled")
        tap0 = sem("tap0")
        tap1, tap2, taps_done = sem("tap1"), sem("tap2"), sem("taps_done")
        silu_done, gated = sem("silu_done"), sem("gated")
        hid_head, hid_ready = sem("hid_head"), sem("hid_ready")
        half_added = sem("half_added")
        u_head, u_ready = sem("u_head"), sem("u_ready")
        sq_done, stat_added = sem("sq_done"), sem("stat_added")
        stat_summed, var_ready, root_ready = sem("stat_summed"), sem("var_ready"), sem("root_ready")
        rstd_ready = sem("rstd_ready")
        consts = sem("consts")
        turned, turned_read = sem("turned"), sem("turned_read")
        pturned, pturned_read = sem("pturned"), sem("pturned_read")
        dve_step, act_step, pool_step = sem("dve_step"), sem("act_step"), sem("pool_step")
        ws_head_ready, ws_ready, ws_done, rtok_turned = sem("ws_head"), sem("ws_ready"), sem("ws_done"), sem("rtok_turned")
        angles_ready, tables_ready = sem("angles_ready"), sem("tables_ready")
        x_ready = sem("x_ready")
        conf_in = sem("conf_in")
        conf_t0, conf_dve, conf_pool = sem("conf_t0"), sem("conf_dve"), sem("conf_pool")
        y_ready = sem("y_ready")
        ln_sum, ln_mean, ln_sub, ln_sq, ln_var, ln_silu, ln_norm = (sem(n) for n in (
            "ln_sum", "ln_mean", "ln_sub", "ln_sq", "ln_var", "ln_silu", "ln_norm"))
        xt_turned, xdt_ready, bt_turned, btok_ready = (sem(n) for n in ("xt_turned", "xdt_ready", "bt_turned", "btok_ready"))
        la_ready, dte_sum, dte_ready, xd2_ready, st_done, st_ready = (sem(n) for n in (
            "la_ready", "dte_sum", "dte_ready", "xd2_ready", "st_done", "st_ready"))
        lat_ready, d_done, e_done, cb_done, cbm_ready, dec_ready, ce_ready, m_ready, ssd_y, y_read = (
            sem(n) for n in ("lat_ready", "d_done", "e_done", "cb_done", "cbm_ready", "dec_ready",
                             "ce_ready", "m_ready", "ssd_y", "y_read"))
        ysq_ready, ynorm_sum, ynorm_var, ynorm_root, ynormed, y_head = (sem(n) for n in (
            "ysq_ready", "ynorm_sum", "ynorm_var", "ynorm_root", "ynormed", "y_head"))
        glu_gate, conv_in, gates_in, rope_in, gates_ready = (sem(n) for n in (
            "glu_gate", "conv_in", "gates_in", "rope_in", "gates_ready"))
        dt_in, dt_exp = sem("dt_in"), sem("dt_exp")
        yc_ready, yc_head, o_head = sem("yc_ready"), sem("yc_head"), sem("o_head")
        swap_ready, kv_ready = sem("swap_ready"), sem("kv_ready")
        vt_turned, vt_ready = sem("vt_turned"), sem("vt_ready")
        blk_ready, h1_done, s1_ready, kc_done, kc_ready, vc_ready = (sem(n) for n in (
            "blk_ready", "h1_done", "s1_ready", "kc_done", "kc_ready", "vc_ready"))
        s_done, s_read, mx_ready, p_ready, pn_ready, pt_done, pt_read, o_done, o_read = (sem(n) for n in (
            "s_done", "s_read", "mx_ready", "p_ready", "pn_ready", "pt_done", "pt_read", "o_done", "o_read"))
        out_gained, last_squared = sem("out_gained"), sem("last_squared")
        out_turned, out_read = sem("out_turned"), sem("out_read")
        store_ready = sem("store_ready")
        tap1_mlp, mask_ready = sem("tap1_mlp"), sem("mask_ready")

        def col(name, i=0):
            return PAR[:, PARAMS[name][0] + i:PARAMS[name][0] + i + 1]

        def dcol(name, i):
            return PAR[:, ds(i + PARAMS[name][0], 1)]

        block = stack.enter_context(nc.Block())

        @block.sync
        def _(sp):
            for t in range(NT):
                sp.dma_start(XST[:, t, :], x[0, t * P:(t + 1) * P, :]).then_inc(x_landed, 16)

            def load_group(weights, s4, units, kt, column, begin=0):
                for u in range(begin, units):
                    if not (isinstance(s4, int) and s4 == 0 and u < RING):
                        sp.wait_ge(cols_done, s4 * (4 * RING) + 4 * (u - RING + 1))
                    src = weights[u * kt * P:(u + 1) * kt * P, column].rearrange("(k p) n -> p k n", p=P)
                    dst = WRAW[:, u % RING, 0:kt * CW].rearrange("p (k n) -> p k n", k=kt)
                    sp.dma_start(dst, src).then_inc(raw_landed[u % RING], 16)

            def load_groups(weights, s, first, n, column):
                step, a = s.units // RING, s.unit // RING + first * (s.units // RING)
                if n > 2:
                    with sp.Fori(0, n) as i:
                        load_group(weights, i * step + a, s.units, s.kt, ds(i * CW + column, CW))
                else:
                    for i in range(n):
                        load_group(weights, i * step + a, s.units, s.kt, ds(i * CW + column, CW))

            def load_mlp(layer):
                up, down = ffn_w_up[layer], ffn_w_down[layer]
                for b, (h0, n) in enumerate(CHUNKS):
                    s = SPANS[f"up{layer}{b}"]
                    with sp.Fori(0, n // 4) as i:
                        for half in range(2):
                            load_group(up, i * 2 + s.unit // RING + half, 4, 4,
                                       ds(i * CW + h0 * P + half * FF, CW))
                    load_groups(down[h0 * P:(h0 + n) * P, :], SPANS[f"down{layer}{b}"], 0, 4, 0)

            s = SPANS["in0"]
            w = ab_w_in[0]
            load_group(w, 0, 1, 4, ds(GLUC, CW))
            sp.wait_ge(par_first, 16 * PAR_FIRST)
            load_group(w, 0, 4, 4, ds(GLUC, CW), begin=1)
            sp.dma_start(WS_RAW[:, :, 0:HEADS], w[:, DTC:DTC + HEADS].rearrange("(k p) n -> p k n", p=P))\
              .then_inc(ws_landed, 16)
            load_groups(w, s, 1, 3, GLUC + CW)
            load_groups(w, s, 4, 2, XBCC + D)
            load_groups(w, s, 6, 4, XBCC)
            load_groups(w, s, 10, 4, ZC)
            load_groups(ab_w_out[0], SPANS["out0"], 0, 4, 0)
            load_mlp(0)
            s = SPANS["in1"]
            w = cd_w_in[0]
            sp.dma_start(WS_RAW[:, :, :], w[:, GATEC:GATEC + NGATE].rearrange("(k p) n -> p k n", p=P))\
              .then_inc(ws_landed, 16)
            load_groups(w, s, 0, 2, KVC)
            sp.dma_start(W1[:, :, :], nsa_cmp_w1[0, 0].rearrange("(l d) o -> d l o", d=HD)).then_inc(w1_landed, 16)
            load_groups(w, s, 2, 4, KVC + 2 * CW)
            load_groups(w, s, 6, 4, QC)
            load_groups(w, s, 10, 4, SC)
            load_groups(w, s, 14, 2, 0)
            load_groups(cd_w_out[0], SPANS["out1"], 0, 4, 0)
            load_mlp(1)
            for j in range(2 * NT):
                t, half = j // 2, ds((j % 2) * (D // 2), D // 2)
                sp.wait_ge(out_read, j + 1)
                sp.wait_ge(store_ready, j + 1)
                sp.dma_start(out[0, t * P:(t + 1) * P, half], OST[:, t, half]).then_inc(stored, 16)
            sp.wait_ge(stored, 16 * 2 * NT)

        @block.gpsimd
        def _(pool):
            steps = [0]

            def link(ins):
                steps[0] += 1
                ins.then_inc(pool_step, 1)
                pool.wait_ge(pool_step, steps[0])

            link(pool.memset(IDENT[:, :], 0.0))
            pool.affine_select(out=IDENT[:, :], in_=IDENT[:, :], compare_op=ALU.not_equal, fill=1.0, base=0,
                               pattern=[[-1, P]], channel_multiplier=1).then_inc(consts, 1)
            pool.memset(ONES[:, :], 1.0).then_inc(consts, 1)
            pool.memset(YP[:, :, :], 0.0).then_inc(consts, 1)
            pool.memset(CP[:, :, 0:CONF_TAPS - 1], 0.0).then_inc(consts, 1)
            pool.wait_ge(consts, 4)
            pool.affine_select(out=TRI[:, :], in_=ONES[:, :], compare_op=ALU.is_ge, fill=0.0, base=0,
                               pattern=[[1, P]], channel_multiplier=-1).then_inc(consts, 1)
            pool.affine_select(out=UST[:, :], in_=ONES[:, :], compare_op=ALU.is_gt, fill=0.0, base=0,
                               pattern=[[-1, P]], channel_multiplier=1).then_inc(consts, 1)
            link(pool.memset(CMPM[:, :, :], 0.0))
            link(pool.memset(CMP1[:, :, :], 1.0))
            for m, fill in ((CMPM, NEG), (CMP1, 0.0)):
                pool.affine_select(out=m[:, :, :], in_=m[:, :, :], compare_op=ALU.is_ge, fill=fill,
                                   base=1 - CB, pattern=[[P, NT], [-CSTRIDE, NCMP]],
                                   channel_multiplier=1).then_inc(consts, 1)
            counts = {"sq": 0, "stat": 0}

            def statistics(tile):
                pool.tensor_tensor(SQ[:, :], H[:, tile, :], H[:, tile, :], ALU.mult).then_inc(sq_done, 1)
                counts["sq"] += 1
                pool.wait_ge(sq_done, counts["sq"])
                if tile == 0:
                    pool.tensor_copy(STAT[:, :], SQ[:, :]).then_inc(stat_added, 1)
                else:
                    pool.tensor_tensor(STAT[:, :], STAT[:, :], SQ[:, :], ALU.add).then_inc(stat_added, 1)
                counts["stat"] += 1
                pool.wait_ge(stat_added, counts["stat"])

            def norm_statistics(n, s):
                if n:
                    pool.wait_ge(stat_summed, n)
                for tile in range(DT - LAST_SQUARES if n == 4 else DT):
                    if s is None:
                        pool.wait_ge(turned_read, tile // 2 + 1)
                    else:
                        pool.wait_ge(bank_read, s.tile + tile + 1)
                    statistics(tile)

            norm_statistics(0, None)
            for m in range(POOL_CONF):
                j = CONF_TILES - POOL_CONF + m
                pool.wait_ge(conf_t0, j + 1)
                for k in range(CONF_TAPS - 1):
                    link(pool.tensor_scalar(SQ[:, :], CP[:, j, k:k + SEQ], col("dw_w", k * CONF_TILES + j), 0.0,
                                            ALU.mult, ALU.add))
                    link(pool.tensor_tensor(CA[:, j, :], CA[:, j, :], SQ[:, :], ALU.add))
                pool.tensor_copy(CA[:, j, :], CA[:, j, :]).then_inc(conf_pool, 1)
            def la_triangle(m):
                g, t = divmod(m, 2)
                if m == 0:
                    pool.wait_ge(cols_done, 4 * SPANS["in0"].unit_end)
                    pool.wait_ge(la_ready, NT)
                if m == 1:
                    pool.wait_ge(ln_norm, CONF_TILES)
                if m >= 2:
                    pool.wait_ge(d_done, m - 1)
                if m >= 2 and t == 1:
                    pool.wait_ge(e_done, m // 2)
                pool.tensor_tensor(LATS[t][:, :].rearrange("p (h l) -> p h l", h=HPG),
                                   LA[:, 32 * t + HPG * g:32 * t + HPG * (g + 1)].unsqueeze(2).to_broadcast([P, HPG, P]),
                                   TRI[:, :].unsqueeze(1).to_broadcast([P, HPG, P]), ALU.mult).then_inc(lat_ready, 1)

            def squares(g):
                pool.wait_ge(y_read, 8 * (g + 1))
                z, y = ZX[:, 4 * g:4 * g + 4, 0:SEQ], ZX[:, 4 * g:4 * g + 4, SEQ:2 * SEQ]
                link(pool.tensor_tensor(y, y, z, ALU.mult))
                link(pool.tensor_tensor(z, y, y, ALU.mult))
                link(pool.tensor_tensor(ZX[:, 4 * g:4 * g + 2, 0:SEQ], ZX[:, 4 * g:4 * g + 2, 0:SEQ],
                                        ZX[:, 4 * g + 2:4 * g + 4, 0:SEQ], ALU.add))
                pool.tensor_tensor(ZX[:, 4 * g, 0:SEQ], ZX[:, 4 * g, 0:SEQ], ZX[:, 4 * g + 1, 0:SEQ],
                                   ALU.add).then_inc(ysq_ready, 1)

            for m in range(4):
                la_triangle(m)
            for g in range(GROUPS):
                if g + 2 < GROUPS:
                    la_triangle(2 * g + 4)
                    la_triangle(2 * g + 5)
                squares(g)
            norm_statistics(1, SPANS["out0"])
            link(pool.memset(MASK[:, :], 0.0))
            pool.affine_select(out=MASK[:, P:2 * P], in_=MASK[:, P:2 * P], compare_op=ALU.is_ge, fill=NEG,
                               base=0, pattern=[[-1, P]], channel_multiplier=1).then_inc(mask_ready, 1)
            norm_statistics(2, SPANS["down02"])
            norm_statistics(3, SPANS["out1"])
            norm_statistics(4, SPANS["down12"])

        @block.scalar
        def _(act):
            rows = (("mix", mix_norm.rearrange("a (t p) -> (a t) p", p=P)),
                    ("ffn", ffn_norm.rearrange("a (t p) -> (a t) p", p=P)),
                    ("final", final_norm.rearrange("(t p) -> t p", p=P)),
                    ("sconv_w", ssm_conv_w[0].rearrange("a (t p) -> (a t) p", p=P)),
                    ("sconv_b", ssm_conv_b[0].rearrange("(t p) -> t p", p=P)),
                    ("snorm", ssm_norm[0].rearrange("(t p) -> t p", p=P)),
                    ("dw_w", conf_dw_w[0].rearrange("a (t p) -> (a t) p", p=P)),
                    ("dw_b", conf_dw_b[0].rearrange("(t p) -> t p", p=P)),
                    ("ln_g", conf_ln_g[0].rearrange("(t p) -> t p", p=P)),
                    ("ln_b", conf_ln_b[0].rearrange("(t p) -> t p", p=P)),
                    ("sc_w", sc_conv_w[0].rearrange("a (t p) -> (a t) p", p=P)),
                    ("pe", nsa_cmp_pe[0].rearrange("a l p -> (a l) p")),
                    ("fconv_w", ffn_conv_w.rearrange("l a (t p) -> (l a t) p", p=P)),
                    ("fconv_b", ffn_conv_b.rearrange("l (t p) -> (l t) p", p=P)))
            loads = 0
            for name, src in rows:
                c0, n = PARAMS[name]
                r = 0
                while r < n:
                    tile, row = divmod(c0 + r, P)
                    k = min(n - r, P - row)
                    act.dma_start(PST[row:row + k, tile, :], src[r:r + k, :])\
                       .then_inc(par_first if tile == 0 else par_landed, 16)
                    r, loads = r + k, loads + 1
            act.dma_start(DTB, ssm_dt_bias[0:1, :].to_broadcast([P, HEADS])).then_inc(misc_landed, 16)
            act.dma_start(ALG, ssm_a_log[0:1, :].to_broadcast([P, HEADS])).then_inc(misc_landed, 16)
            act.dma_start(DALL, ssm_d[0:1, :].to_broadcast([P, HEADS])).then_inc(misc_landed, 16)
            act.dma_start(POSI[:, :], positions[0:1, :].to_broadcast([P, SEQ])).then_inc(misc_landed, 16)
            act.dma_start(INV, inv_freq).then_inc(misc_landed, 16)
            assert loads == PAR_LOADS

            steps = [0]

            def link(ins):
                steps[0] += 1
                ins.then_inc(act_step, 1)
                act.wait_ge(act_step, steps[0])

            def heads(s4, off, kt=4):
                act.wait_ge(raw_landed[off % RING], s4 * 16 + 16 * (off // RING + 1))
                act.activation(WHEAD[:, off % RING, 0:kt * CW], WRAW[:, off % RING, 0:kt * CW], ACT.Copy)\
                   .then_inc(heads_ready, 1)

            def copy_halves(e):
                for c in range(4):
                    act.wait_ge(cols_done, e * 4 + c - 3)
                    act.activation(TMP[:, c, :], bank[c][:, SEQ:2 * SEQ], ACT.Copy).then_inc(half_copied, 1)

            def u_heads(gain, tile):
                act.activation(U[:, tile, 0:SEQ], H[:, tile, :], ACT.Copy, scale=gain).then_inc(u_head, 1)

            def root(n):
                act.wait_ge(var_ready, n)
                act.activation(ROOT, RSTD[:, :], ACT.Sqrt).then_inc(root_ready, 1)
                act.wait_ge(rstd_ready, n)

            act.wait_ge(pturned, 1)
            act.activation(PAR[:, 0:P], bank[0][:, 0:P], ACT.Copy).then_inc(pturned_read, 1)

            def parameters():
                for b in range(PBANKS):
                    act.wait_ge(pturned, b + 2)
                    w = min(4 * P, NPARAM - (4 * b + 1) * P)
                    act.activation(PAR[:, (4 * b + 1) * P:(4 * b + 1) * P + w], bank[5 + b][:, 0:w], ACT.Copy)\
                       .then_inc(pturned_read, 1)

            for tile in range(DT):
                if tile % 4 == 0:
                    heads(0, tile // 4)
                if tile == 0:
                    act.wait_ge(pturned_read, 1)
                act.wait_ge(turned_read, tile // 2 + 1)
                u_heads(col("mix", tile), tile)
            heads(0, 4)
            root(1)
            heads(0, 5)

            def mlp(layer):
                for b, (h0, n) in enumerate(CHUNKS):
                    s, gate0 = SPANS[f"up{layer}{b}"], layer * FT + h0
                    plain, conv = PLAIN[f"up{layer}{b}"], CONV[f"up{layer}{b}"]

                    def turn(i, turns):
                        for half in range(2):
                            first = s.unit + 4 * half + 4
                            kts = ahead(first + (8 * i if turns == 1 else 0), 8, turns)
                            e = i * 8 + first
                            e4 = i * 2 + (s.unit // RING + half + 1)
                            copy_halves(e)
                            heads(e4, 2, kts[0])
                            for c in range(4):
                                k = i * 8 + (4 * half + c + 1)
                                t = i * 4 + (h0 + c + half * FT)
                                act.wait_ge(scaled, k + plain)
                                act.activation(ACC[:, c, :], YP[:, c, 3:3 + SEQ], ACT.Identity,
                                               bias=dcol("fconv_b", t + layer * 2 * FT),
                                               scale=dcol("fconv_w", t + (layer * 3 + 2) * 2 * FT))\
                                   .then_inc(tap0, 1)
                            heads(e4, 3, kts[1])
                            for c in range(4):
                                if half == 0:
                                    act.wait_ge(taps_done, i * 8 + (conv + c + 1))
                                    act.activation(SG[:, c, :], ACC[:, c, :], ACT.Silu).then_inc(silu_done, 1)
                                else:
                                    act.wait_ge(gated, i * 4 + (gate0 + c + 1))
                                    act.activation(Y[:, ds(i * 4 + c, 1), 0:SEQ], ACC[:, c:c + 1, :], ACT.Copy)\
                                       .then_inc(hid_head, 1)
                            heads(e4, 4, kts[2])
                            heads(e4, 5, kts[3])

                    turns = n // 4 - (b == len(CHUNKS) - 1)
                    with act.Fori(0, turns) as i:
                        turn(i, turns)
                    if turns < n // 4:
                        turn(turns, 1)
                    s = SPANS[f"down{layer}{b}"]
                    last = b == len(CHUNKS) - 1
                    norm = 2 * layer + 2
                    if last:
                        gain = ("mix", DT) if layer == 0 else ("final", 0)
                        residual_groups(s, 2, gain)
                        for i in (2, 3):
                            e = s.unit + 4 * (i + 1)
                            residual_group(s.tile + 4 * i, e, e // RING, i, gain, rest(e),
                                           norm + 1 if i == 3 and layer == 0 else None)
                    else:
                        residual_groups(s, 4, None)

            def residual_group(t, e, e4, i, gain, kts, norm=None):
                for k, kt in enumerate(kts):
                    if norm is not None and k == 3:
                        root(norm)
                    heads(e4, k + 2, kt)
                    if k == 0 and gain is not None and gain[0] != "final":
                        for c in range(4):
                            act.wait_ge(bank_read, t + c + 1)
                            tile = i * 4 + c
                            act.activation(U[:, ds(tile, 1), 0:SEQ], H[:, ds(tile, 1), :], ACT.Copy,
                                           scale=dcol(gain[0], i * 4 + (c + gain[1]))).then_inc(u_head, 1)
                if gain is not None and gain[0] == "final":
                    for c in range(4):
                        act.wait_ge(bank_read, t + c + 1)
                        tile = i * 4 + c
                        if isinstance(tile, int) and tile >= DT - LAST_SQUARES:
                            act.activation(TMP[:, 4 + tile - DT, :], H[:, tile, :], ACT.Square).then_inc(last_squared, 1)
                        act.activation(HG[:, ds(tile, 1), :], H[:, ds(tile, 1), :], ACT.Copy,
                                       scale=dcol("final", tile)).then_inc(out_gained, 1)

            def residual_groups(s, n, gain):
                kts = ahead(s.unit + s.units, s.units, n)
                with act.Fori(0, n) as i:
                    residual_group(i * 4 + s.tile, i * s.units + (s.unit + s.units),
                                   i * (s.units // RING) + (s.unit + s.units) // RING, i, gain, kts)

            def out_projection(layer):
                s = SPANS[f"out{layer}"]
                for i in range(s.groups):
                    e = s.unit + (i + 1) * s.units
                    kts = ahead(e, 0, 1, range(2, 10 if i < 3 else 6))
                    residual_group(s.tile + 4 * i, e, e // RING, i, ("ffn", layer * DT), kts,
                                   2 * layer + 2 if i == 3 else None)

            def small_heads(n):
                act.wait_ge(ws_landed, 16 * (1 if n == HEADS else 2))
                act.activation(WS_HEAD[:, :, 0:n], WS_RAW[:, :, 0:n], ACT.Copy).then_inc(ws_head_ready, 1)

            s, conv, ready = SPANS["in0"], 0, 0
            small_heads(HEADS)
            for q in range(s.groups):
                e = s.unit + 4 * (q + 1)
                last = q == s.groups - 1
                copy_halves(e)
                kts = ahead(e, 0, 1)
                if not last:
                    heads(e // RING, 2, kts[0])
                for c in range(4):
                    done = PLAIN["in0"] + 4 * q + c + 1
                    if 4 <= q < 10:
                        j = (16 + 4 * (q - 4) if q < 6 else 4 * (q - 6)) + c
                        act.wait_ge(scaled, done)
                        act.activation(ACC[:, c, :], YP[:, c, 3:3 + SEQ], ACT.Identity,
                                       bias=col("sconv_b", j), scale=col("sconv_w", 3 * 24 + j)).then_inc(tap0, 1)
                if not last:
                    heads(e // RING, 3, kts[1])
                for c in range(4):
                    done = PLAIN["in0"] + 4 * q + c + 1
                    if 2 <= q < 4:
                        act.wait_ge(scaled, done)
                        act.activation(SG[:, c, :], YP[:, c, 3:3 + SEQ], ACT.Sigmoid).then_inc(glu_gate, 1)
                    elif 4 <= q < 10:
                        conv += 1
                        act.wait_ge(taps_done, conv)
                        dst = BC[:, 4 * (q - 4) + c, :] if q < 6 else ZX[:, 4 * (q - 6) + c, SEQ:2 * SEQ]
                        act.activation(dst, ACC[:, c, :], ACT.Silu).then_inc(x_ready, 1)
                    elif q >= 10:
                        act.wait_ge(scaled, done)
                        act.activation(ZX[:, 4 * (q - 10) + c, 0:SEQ], YP[:, c, 3:3 + SEQ], ACT.Silu)\
                           .then_inc(x_ready, 1)
                if q in (2, 3):
                    for c in range(4):
                        j = 4 * (q - 2) + c
                        act.wait_ge(conf_in, j + 1)
                        act.activation(CA[:, j, :], CP[:, j, CONF_TAPS - 1:CONF_TAPS - 1 + SEQ], ACT.Identity,
                                       bias=col("dw_b", j), scale=col("dw_w", (CONF_TAPS - 1) * CONF_TILES + j))\
                           .then_inc(conf_t0, 1)
                if q == 5:
                    act.wait_ge(dte_sum, 1)
                    act.activation(DTE, bank[6][:, 0:HEADS], ACT.Exp).then_inc(dte_ready, 1)
                if q == 11:
                    act.wait_ge(bt_turned, 1)
                    act.activation(BTOK[:, :, :], bank[7][:, :].rearrange("p (g n) -> p g n", g=GROUPS), ACT.Copy)\
                       .then_inc(btok_ready, 1)
                    act.wait_ge(ln_sum, 1)
                    act.activation(LNM, bank[4][:, 0:SEQ], ACT.Copy, scale=1.0 / (CONF_TILES * P)).then_inc(ln_mean, 1)
                    act.wait_ge(ln_sub, 1)
                    act.activation(CP[:, :, 0:SEQ], CA[:, :, :], ACT.Square).then_inc(ln_sq, 1)
                if q == 12:
                    act.wait_ge(ln_var, 1)
                    act.activation(LNR, LNM, ACT.Sqrt).then_inc(ln_var, 1)
                    for j in range(CONF_TILES):
                        act.wait_ge(ln_norm, j + 1)
                        act.activation(CA[:, j, :], CA[:, j, :], ACT.Silu, bias=col("ln_b", j)).then_inc(ln_silu, 1)
                    act.wait_ge(ln_silu, CONF_TILES)
                    act.activation(Y[:, SSM_TILES:SSM_TILES + CONF_TILES, 0:SEQ], CA[:, :, :], ACT.Copy)\
                       .then_inc(ln_mean, 1)
                if q == 0:
                    parameters()
                if q == 2:
                    act.wait_ge(angles_ready, 1)
                    act.activation(SIN[:, :], SIN[:, :], ACT.Sin).then_inc(tables_ready, 1)
                    act.activation(COS[:, :], COS[:, :], ACT.Sin).then_inc(tables_ready, 1)
                    act.wait_ge(dt_in, 1)
                    act.activation(S2, S2, ACT.Exp).then_inc(dt_exp, 1)
                    act.wait_ge(misc_landed, 16 * 5)
                    act.activation(AN, ALG, ACT.Exp).then_inc(dt_exp, 1)
                if not last:
                    heads(e // RING, 4, kts[2])
                    heads(e // RING, 5, kts[3])


            def group_root(g):
                act.wait_ge(ynorm_var, g + 1)
                act.activation(YS, YV[:, :], ACT.Sqrt).then_inc(ynorm_root, 1)

            def group_heads(g):
                act.wait_ge(ynormed, 4 * g + 4)
                act.activation(Y[:, 4 * g:4 * g + 4, 0:SEQ], ZX[:, 4 * g:4 * g + 4, SEQ:2 * SEQ], ACT.Copy)\
                   .then_inc(y_head, 1)

            for m in range(2 * GROUPS):
                g, chunk = divmod(m, 2)
                act.wait_ge(d_done, m + 1)
                if m >= 2:
                    act.wait_ge(ssd_y, m - 1)
                for h in range(2):
                    act.activation(DEC[:, m % 2, h * 512:(h + 1) * 512], bank[4 + h][:, :], ACT.Exp).then_inc(dec_ready, 1)
                if chunk == 0:
                    act.wait_ge(st_done, g + 1)
                    if g:
                        act.wait_ge(ssd_y, 2 * g)
                    act.activation(ST[:, :], bank[3][:, :], ACT.Copy).then_inc(st_ready, 1)
                else:
                    act.wait_ge(e_done, g + 1)
                    if g:
                        act.wait_ge(ssd_y, 2 * g)
                    for h in range(2):
                        act.activation(CE[:, h * 512:(h + 1) * 512], bank[h][:, :], ACT.Exp).then_inc(dec_ready, 1)
                if m in (0, 1):
                    heads(e // RING, m + 2, kts[m])
                if m in (4, 6):
                    group_root(m // 2 - 2)
                if m == 6:
                    group_heads(0)
            group_heads(1)
            group_root(2)
            group_heads(2)
            group_root(3)
            group_heads(3)
            e = SPANS["out0"].unit
            for k in range(4, 10):
                heads(e // RING, k, kt_at(e + k))
            out_projection(0)
            mlp(0)

            s = SPANS["in1"]
            small_heads(NGATE)

            def compress_silu(i):
                act.wait_ge(h1_done, i + 1)
                if i == 0:
                    act.dma_start(W1[:, :, :], nsa_cmp_w1[0, 1].rearrange("(l d) o -> d l o", d=HD))\
                       .then_inc(w1_landed, 16)
                act.activation(S1K, bank[4][:, 0:KVH * NCMP], ACT.Silu).then_inc(s1_ready, 1)

            def compressed_k():
                act.wait_ge(kc_done, 1)
                act.activation(KC0, bank[5][:, 0:KVH * NCMP], ACT.Copy).then_inc(kc_ready, 1)
                act.activation(KSW[0:64, :], bank[5][64:128, 0:KVH * NCMP], ACT.Copy).then_inc(kc_ready, 1)
                act.activation(KSW[64:128, :], bank[5][0:64, 0:KVH * NCMP], ACT.Copy).then_inc(kc_ready, 1)

            def compressed_v():
                act.wait_ge(kc_done, 2)
                act.wait_ge(kv_ready, 4 * 6 + 1)
                act.activation(VCT, bank[5][0:NCMP, 0:KVH * HD], ACT.Copy).then_inc(vc_ready, 1)

            for q in range(s.groups):
                e = s.unit + 4 * (q + 1)
                copy_halves(e)
                kts = ahead(e, 0, 1)
                last = q == s.groups - 1
                if not last:
                    heads(e // RING, 2, kts[0])
                if q in (2, 4, 6, 7, 8, 9):
                    for c in range(4):
                        act.wait_ge(scaled, PLAIN["in1"] + 4 * q + c + 1)
                        act.activation(SG[0:64, c, :], YP[64:128, c, 3:3 + SEQ], ACT.Copy).then_inc(swap_ready, 1)
                        act.activation(SG[64:128, c, :], YP[0:64, c, 3:3 + SEQ], ACT.Copy).then_inc(swap_ready, 1)
                if q in (12, 13):
                    for c in range(4):
                        j = 4 * (q - 12) + c
                        act.wait_ge(conv_in, j + 1)
                        act.activation(ACC[:, c, :], YP[:, c, 3:3 + SEQ], ACT.Copy,
                                       scale=col("sc_w", 2 * 8 + j)).then_inc(tap0, 1)
                if not last:
                    heads(e // RING, 3, kts[1])
                if q in (14, 15):
                    act.wait_ge(yc_ready, 4 * (q - 13))
                    act.activation(Y[:, 4 * (q - 14):4 * (q - 14) + 4, 0:SEQ], ACC[:, :, :], ACT.Copy)\
                       .then_inc(yc_head, 1)
                if q == 2:
                    act.wait_ge(gates_in, 1)
                    act.activation(GT, GT, ACT.Sigmoid).then_inc(gates_ready, 1)
                    act.dma_start(W2.rearrange("p (i n) -> p i n", i=2), nsa_cmp_w2[0].rearrange("i p n -> p i n"))\
                       .then_inc(w2_landed, 16)
                if q == COMPRESS[0] + 1:
                    compress_silu(0)
                if q == COMPRESS[1] + 1:
                    compressed_k()
                    compress_silu(1)
                if q == 10:
                    compressed_v()
                if q < s.groups - 1:
                    heads(e // RING, 4, kts[2])
                    heads(e // RING, 5, kts[3])

            for k in range(4):
                act.wait_ge(vt_turned, k + 1)
                act.activation(VTOK[:, k % 2, 4 * (k // 2):4 * (k // 2) + 4, :],
                               bank[4 + k][:, :].rearrange("p (g d) -> p g d", g=KVH), ACT.Copy).then_inc(vt_ready, 1)
            last = NSA_HEADS * NT
            for n in range(last + 5):
                if n in (5, 9):
                    heads(e // RING, n // 4 + 1, kts[n // 4 - 1])
                if 2 <= n < last + 2:
                    m = n - 2
                    blocks = 2 * (m % NT + 1)
                    act.wait_ge(pt_done, m + 1)
                    if m >= 2:
                        act.wait_ge(o_done, m - 1)
                    act.activation(PT[:, m % 2, 0:blocks * P], bank[4 + m % 2][:, 0:blocks * P], ACT.Copy).then_inc(pt_read, 1)
                    act.activation(PTC[0:NCMP, m % 2, :], bank[3 - m % 2][0:NCMP, P:2 * P], ACT.Copy).then_inc(pt_read, 1)
                if n < last:
                    b, p3, nk = n % 2, n % 3, P * (n % NT + 1)
                    act.wait_ge(mx_ready, n + 1)
                    for r, probs in enumerate((PROB[:, p3, 512:512 + NCMP], PROB[:, p3, 0:nk], PROB[:, p3, SEQ:SEQ + nk])):
                        act.activation(probs, probs, ACT.Exp, bias=MX[:, 4 * b + r:4 * b + r + 1], scale=SCALE,
                                       accum_out=SUMS[:, 4 * b + r:4 * b + r + 1]).then_inc(p_ready, 1)
                if n >= 6 and n % NT == 0:
                    h = n // NT - 3
                    act.wait_ge(o_done, NT * (h + 1))
                    act.activation(Y[:, 8 + h, 0:SEQ], bank[6 + h % 2][:, 0:SEQ], ACT.Copy).then_inc(o_head, 1)
            e = SPANS["out1"].unit
            for k in range(4, 10):
                heads(e // RING, k, kt_at(e + k))
            out_projection(1)
            mlp(1)

            act.wait_ge(var_ready, 5)
            act.activation(RSQ, RVAR, ACT.Sqrt).then_inc(root_ready, 1)
            act.wait_ge(rstd_ready, 5)
            for k in range(1, 4 * NT, 2):
                act.wait_ge(out_turned, k + 1)
                act.activation(OST[:, k // 4, (k % 4) * 512:(k % 4 + 1) * 512], bank[4 + k % 4][:, :], ACT.Copy,
                               scale=RTOK[:, k // 4:k // 4 + 1]).then_inc(store_ready, 1)

        @block.vector
        def _(dve):
            steps = [0]

            def link(ins):
                steps[0] += 1
                ins.then_inc(dve_step, 1)
                dve.wait_ge(dve_step, steps[0])

            def tails(n, off, kt=4):
                dve.wait_ge(heads_ready, n + off + 1)
                dve.tensor_tensor(WTAIL[:, off % RING, 0:kt * CW], WRAW[:, off % RING, 0:kt * CW],
                                  WHEAD[:, off % RING, 0:kt * CW].bitcast(F32), ALU.subtract).then_inc(tails_ready, 1)

            def read_banks(plain, tile, dst):
                for c in range(4):
                    dve.wait_ge(half_copied, plain + c + 1)
                    dve.tensor_tensor(TMP[:, c, :], bank[c][:, 0:SEQ], TMP[:, c, :], ALU.add).then_inc(bank_read, 1)
                    dve.wait_ge(bank_read, tile + c + 1)
                    dve.tensor_tensor(dst(c), TMP[:, c, :], RSTD[:, :], ALU.mult).then_inc(scaled, 1)

            def data(c):
                return YP[:, c, 3:3 + SEQ]

            def back(c, k):
                return YP[:, c, 3 - k:3 - k + SEQ]

            def newton(v, y, t, result):
                link(dve.reciprocal(y, y))
                link(dve.tensor_tensor(t, y, y, ALU.mult))
                link(dve.tensor_tensor(t, t, v, ALU.mult))
                link(dve.tensor_scalar(t, t, -0.5, 1.5, ALU.mult, ALU.add))
                return dve.tensor_tensor(result, y, t, ALU.mult)

            def variance(n):
                dve.wait_ge(stat_summed, n)
                dve.tensor_scalar(RSTD[:, :], bank[4][:, 0:SEQ], 1.0 / D, EPS, ALU.mult, ALU.add).then_inc(var_ready, 1)

            def norm_factor(n):
                dve.wait_ge(root_ready, n)
                newton(RSTD[:, :], ROOT, NEWT, RSTD[:, :]).then_inc(rstd_ready, 1)
                dve.wait_ge(rstd_ready, n)

            for k in range(8):
                dve.wait_ge(turned, k + 1)
                dve.tensor_copy(H[:, 2 * k:2 * k + 2, :], bank[4 + k % 4][:, :].rearrange("p (j s) -> p j s", j=2))\
                   .then_inc(turned_read, 1)
            for tile in range(DT):
                if tile % 4 == 0:
                    tails(0, tile // 4)
                dve.wait_ge(u_head, tile + 1)
                dve.scalar_tensor_tensor(out=U[:, tile, SEQ:2 * SEQ], in0=H[:, tile, :], scalar=col("mix", tile),
                                         in1=U[:, tile, 0:SEQ].bitcast(F32), op0=ALU.mult, op1=ALU.subtract)\
                   .then_inc(u_ready, 1)
            tails(0, 4)
            variance(1)
            norm_factor(1)
            tails(0, 5)

            def rotary_angles():
                dve.wait_ge(misc_landed, 16 * 5)
                for r in range(2):
                    half = slice(HP * r, HP * (r + 1))
                    link(dve.tensor_copy(DSK[half, :], DALL[half, r:HEADS:2]))

                dve.wait_ge(misc_landed, 16 * 5)
                a, k = ACC[:, 1, :], ACC[:, 2, :]
                link(dve.tensor_copy(ACC[:, 0, :], POSI[:, :]))
                link(dve.tensor_scalar(a, ACC[:, 0, :], INV, None, ALU.mult))
                link(dve.tensor_scalar(k, a, float(0.5 / np.pi), ROUNDER, ALU.mult, ALU.add))
                link(dve.tensor_scalar(k, k, ROUNDER, None, ALU.subtract))
                for part in TURN:
                    link(dve.scalar_tensor_tensor(out=a, in0=k, scalar=-part, in1=a, op0=ALU.mult, op1=ALU.add))
                link(dve.tensor_scalar(a, a, PI, -PI, ALU.min, ALU.max))
                link(dve.scalar_tensor_tensor(out=k, in0=a, scalar=-1.0, in1=a, op0=ALU.mult, op1=ALU.max))
                link(dve.tensor_scalar(SIN[0:64, :], a[0:64, :], -1.0, None, ALU.mult))
                link(dve.tensor_copy(SIN[64:128, :], a[64:128, :]))
                dve.tensor_scalar(COS[:, :], k, -1.0, float(np.float32(np.pi / 2)), ALU.mult, ALU.add).then_inc(angles_ready, 1)

            def small_tails(count, n):
                dve.wait_ge(ws_head_ready, count)
                dve.tensor_tensor(WS_TAIL[:, :, 0:n], WS_RAW[:, :, 0:n], WS_HEAD[:, :, 0:n].bitcast(F32),
                                  ALU.subtract).then_inc(ws_ready, 1)

            def small_scaled(count, n, dst):
                dve.wait_ge(rtok_turned, count)
                link(dve.tensor_copy(RTOK, bank[5][:, 0:2 * P:P]))
                for t in range(NT):
                    link(dve.tensor_scalar(dst[:, t * n:(t + 1) * n], bank[4][:, 64 * t:64 * t + n],
                                           RTOK[:, t:t + 1], None, ALU.mult))

            def step_sizes():
                small_scaled(1, HEADS, S1)
                for t in range(NT):
                    link(dve.tensor_tensor(S1[:, 32 * t:32 * t + 32], S1[:, 32 * t:32 * t + 32], DTB, ALU.add))
                dve.scalar_tensor_tensor(out=S2, in0=S1, scalar=-1.0, in1=S1, op0=ALU.mult, op1=ALU.min)\
                   .then_inc(dt_in, 1)

            def step_sizes_end():
                dve.wait_ge(dt_exp, 2)
                link(dve.tensor_scalar(S3, S2, 2.0, None, ALU.add))
                link(dve.reciprocal(S3, S3))
                link(dve.tensor_tensor(S3, S2, S3, ALU.mult))
                link(dve.tensor_tensor(S4, S3, S3, ALU.mult))
                link(dve.tensor_scalar(S2, S4, 1.0 / 17, None, ALU.mult))
                for odd in (15, 13, 11, 9, 7, 5, 3):
                    link(dve.scalar_tensor_tensor(out=S2, in0=S2, scalar=1.0 / odd, in1=S4, op0=ALU.add, op1=ALU.mult))
                link(dve.tensor_scalar(S2, S2, 1.0, 2.0, ALU.add, ALU.mult))
                link(dve.tensor_tensor(S2, S2, S3, ALU.mult))
                link(dve.scalar_tensor_tensor(out=DTV, in0=S1, scalar=0.0, in1=S2, op0=ALU.max, op1=ALU.add))
                for t in range(NT):
                    r = slice(32 * t, 32 * t + 32)
                    dve.scalar_tensor_tensor(out=LA[:, r], in0=DTV[:, r], scalar=-1.0, in1=AN, op0=ALU.mult,
                                             op1=ALU.mult).then_inc(la_ready, 1)
                dve.wait_ge(la_ready, NT)

            small_tails(1, HEADS)
            s, conv, conf, n_conf = SPANS["in0"], 0, 0, CONF_TILES - POOL_CONF
            conf_ops = [(k, j) for k in range(CONF_TAPS - 1) for j in range(n_conf)]
            dve.wait_ge(consts, CONSTS)
            for q in range(s.groups):
                e, last = s.unit + 4 * (q + 1), q == s.groups - 1
                dst = data if q > 1 else lambda c: CA[:, 4 * q + c, :]
                read_banks(PLAIN["in0"] + 4 * q, s.tile + 4 * q, dst)
                if last:
                    break
                kts = ahead(e, 0, 1)
                tails(e, 2, kts[0])
                if q in (2, 3):
                    for c in range(4):
                        j = 4 * (q - 2) + c
                        dve.wait_ge(glu_gate, j + 1)
                        dve.tensor_tensor(CP[:, j, CONF_TAPS - 1:CONF_TAPS - 1 + SEQ], CA[:, j, :], SG[:, c, :],
                                          ALU.mult).then_inc(conf_in, 1)
                if 4 <= q < 10:
                    j0 = 16 + 4 * (q - 4) if q < 6 else 4 * (q - 6)
                    for k, done in ((1, tap1), (2, tap2), (3, taps_done)):
                        before = (tap0, tap1, tap2)[k - 1]
                        for c in range(4):
                            dve.wait_ge(before, conv + c + 1)
                            dve.scalar_tensor_tensor(out=ACC[:, c, :], in0=back(c, k),
                                                     scalar=col("sconv_w", (3 - k) * 24 + j0 + c), in1=ACC[:, c, :],
                                                     op0=ALU.mult, op1=ALU.add).then_inc(done, 1)
                    conv += 4
                tails(e, 3, kts[1])
                if q == 1:
                    rotary_angles()
                if q == 2:
                    step_sizes()
                if q == 3:
                    step_sizes_end()
                if 3 <= q < 11:
                    share = {3: len(conf_ops) // 20, 10: len(conf_ops) // 4}.get(q, -(-len(conf_ops) * 7 // 60))
                    for k, j in conf_ops[conf:conf + share]:
                        if k == 0:
                            dve.wait_ge(conf_t0, j + 1)
                        else:
                            dve.wait_ge(conf_dve, conf + 1 - n_conf)
                        dve.scalar_tensor_tensor(out=CA[:, j, :], in0=CP[:, j, k:k + SEQ],
                                                 scalar=col("dw_w", k * CONF_TILES + j), in1=CA[:, j, :],
                                                 op0=ALU.mult, op1=ALU.add).then_inc(conf_dve, 1)
                        conf += 1
                if q == 11:
                    assert conf == len(conf_ops)
                    dve.wait_ge(ln_mean, 1)
                    dve.tensor_tensor(CA[:, :, :], CA[:, :, :], LNM.unsqueeze(1).to_broadcast([P, CONF_TILES, SEQ]),
                                      ALU.subtract).then_inc(ln_sub, 1)
                if q == 12:
                    dve.wait_ge(ln_sum, 2)
                    dve.tensor_scalar(LNM, bank[5][:, 0:SEQ], 1.0 / (CONF_TILES * P), EPS, ALU.mult, ALU.add)\
                       .then_inc(ln_var, 1)
                    dve.wait_ge(ln_var, 2)
                    link(newton(LNM, LNR, LNF, LNF))
                    for j in range(CONF_TILES):
                        dve.scalar_tensor_tensor(out=CA[:, j, :], in0=CA[:, j, :], scalar=col("ln_g", j), in1=LNF,
                                                 op0=ALU.mult, op1=ALU.mult).then_inc(ln_norm, 1)
                tails(e, 4, kts[2])
                tails(e, 5, kts[3])

            def x_dt(k):
                g, t = divmod(k, 2)
                dve.wait_ge(xt_turned, k + 1)
                dve.tensor_tensor(XDT[:, t, g * 512:(g + 1) * 512].rearrange("p (h c) -> p h c", h=HPG),
                                  bank[4 + k % 4][:, :].rearrange("p (h c) -> p h c", h=HPG),
                                  DTV[:, 32 * t + HPG * g:32 * t + HPG * (g + 1)].unsqueeze(2).to_broadcast([P, HPG, HP]),
                                  ALU.mult).then_inc(xdt_ready, 1)

            for k in range(2 * GROUPS):
                x_dt(k)

            def x_dt_end(g):
                if g:
                    dve.wait_ge(st_done, g)
                dve.tensor_tensor(XD2[:, :].rearrange("p (h c) -> p h c", h=HPG),
                                  XDT[:, 0, g * 512:(g + 1) * 512].rearrange("p (h c) -> p h c", h=HPG),
                                  DTE[:, HPG * g:HPG * (g + 1)].unsqueeze(2).to_broadcast([P, HPG, HP]),
                                  ALU.mult).then_inc(xd2_ready, 1)

            def cb_masked(m):
                dve.wait_ge(cb_done, m + 1)
                if m >= 2:
                    dve.wait_ge(m_ready, m - 1)
                dve.tensor_tensor(CBM[:, m % 2, :], bank[2][:, 0:P], TRI[:, :], ALU.mult).then_inc(cbm_ready, 1)
                dve.wait_ge(cbm_ready, m + 1)

            def heads_of(buf):
                return buf.rearrange("p (h l) -> p h l", h=HPG)

            def read_y(m):
                g, t = divmod(m, 2)
                dve.wait_ge(ssd_y, m + 1)
                for j in range(4):
                    xs = ZX[:, 4 * g + j, SEQ + t * P:SEQ + (t + 1) * P]
                    dve.scalar_tensor_tensor(out=xs, in0=xs, scalar=DSK[:, 4 * g + j:4 * g + j + 1],
                                             in1=bank[6 + t][:, j * P:(j + 1) * P], op0=ALU.mult, op1=ALU.add)\
                       .then_inc(y_read, 1)

            def group_variance(g):
                dve.wait_ge(ynorm_sum, g + 1)
                src = bank[2][:, SEQ:2 * SEQ] if g < 2 else bank[7 - g][:, 0:SEQ]
                dve.tensor_scalar(YV[:, :], src, 1.0 / (4 * P), EPS, ALU.mult, ALU.add).then_inc(ynorm_var, 1)

            def group_norm(g):
                dve.wait_ge(ynorm_root, g + 1)
                link(newton(YV[:, :], YS, YT[:, :], YT[:, :]))
                for j in range(4 * g, 4 * g + 4):
                    y = ZX[:, j, SEQ:2 * SEQ]
                    dve.scalar_tensor_tensor(out=y, in0=y, scalar=col("snorm", j), in1=YT[:, :],
                                             op0=ALU.mult, op1=ALU.mult).then_inc(ynormed, 1)

            def group_tails(g):
                dve.wait_ge(y_head, g + 1)
                y = Y[:, 4 * g:4 * g + 4, :]
                dve.tensor_tensor(y[:, :, SEQ:2 * SEQ], ZX[:, 4 * g:4 * g + 4, SEQ:2 * SEQ],
                                  y[:, :, 0:SEQ].bitcast(F32), ALU.subtract).then_inc(y_ready, 1)

            e = SPANS["out0"].unit
            dve.wait_ge(dte_ready, 1)
            dve.wait_ge(xdt_ready, 2 * GROUPS)
            x_dt_end(0)
            cb_masked(0)
            exps = 0
            for m in range(2 * GROUPS):
                g, t = divmod(m, 2)
                if m in (4, 6):
                    group_variance(m // 2 - 2)
                if m == 7:
                    group_tails(0)
                exps += 2
                dve.wait_ge(dec_ready, exps)
                dec = heads_of(DEC[:, m % 2, :])
                dve.tensor_tensor(dec, dec, CBM[:, m % 2, :].unsqueeze(1).to_broadcast([P, HPG, P]), ALU.mult).then_inc(m_ready, 1)
                if m + 1 < 2 * GROUPS:
                    cb_masked(m + 1)
                if t == 1:
                    exps += 2
                    dve.wait_ge(dec_ready, exps)
                    ce = heads_of(CE[:, :])
                    dve.tensor_tensor(ce, ce, BC[:, 4 + g, P:2 * P].unsqueeze(1).to_broadcast([P, HPG, P]),
                                      ALU.mult).then_inc(ce_ready, 1)
                elif g + 1 < GROUPS:
                    x_dt_end(g + 1)
                if m:
                    read_y(m - 1)
                if m == 0:
                    tails(e, 2, kt_at(e + 2))
                if m == 1:
                    tails(e, 3, kt_at(e + 3))
                if m == 2:
                    dve.wait_ge(ln_mean, 2)
                    conf = Y[:, SSM_TILES:SSM_TILES + CONF_TILES, :]
                    dve.tensor_tensor(conf[:, :, SEQ:2 * SEQ], CA[:, :, :], conf[:, :, 0:SEQ].bitcast(F32),
                                      ALU.subtract).then_inc(y_ready, 1)
                if m in (5, 7):
                    group_norm((m - 5) // 2)
            read_y(2 * GROUPS - 1)
            group_tails(1)
            group_variance(2)
            group_norm(2)
            group_tails(2)
            group_variance(3)
            group_norm(3)
            group_tails(3)
            for k in range(4, 10):
                tails(e, k, kt_at(e + k))

            def residual_group(t, halves, e, i, gain, uready, kts, norm=None):
                for c in range(4):
                    dve.wait_ge(cols_done, e * 4 + c - 3)
                    h = H[:, ds(i * 4 + c, 1), :]
                    dve.tensor_tensor(h, bank[c][:, 0:SEQ].unsqueeze(1), h, ALU.add).then_inc(half_added, 1)
                    dve.wait_ge(half_added, halves + c + 1)
                    dve.tensor_tensor(h, bank[c][:, SEQ:2 * SEQ].unsqueeze(1), h, ALU.add).then_inc(bank_read, 1)
                for k, kt in enumerate(kts):
                    if norm is not None and k == 3:
                        variance(norm)
                        norm_factor(norm)
                    tails(e, k + 2, kt)
                    if k == 0 and gain is not None:
                        for c in range(4):
                            dve.wait_ge(u_head, uready + c + 1)
                            u = U[:, ds(i * 4 + c, 1), :]
                            dve.scalar_tensor_tensor(out=u[:, :, SEQ:2 * SEQ], in0=H[:, ds(i * 4 + c, 1), :],
                                                     scalar=dcol(gain[0], i * 4 + (c + gain[1])),
                                                     in1=u[:, :, 0:SEQ].bitcast(F32), op0=ALU.mult, op1=ALU.subtract)\
                               .then_inc(u_ready, 1)

            def residual_groups(name, n, gain, uready):
                s = SPANS[name]
                kts = ahead(s.unit + s.units, s.units, n)
                with dve.Fori(0, n) as i:
                    residual_group(i * 4 + s.tile, i * 4 + HALVES[name], i * s.units + (s.unit + s.units), i, gain,
                                   i * 4 + uready, kts)

            def out_projection(layer):
                name = f"out{layer}"
                s = SPANS[name]
                for i in range(s.groups):
                    e = s.unit + (i + 1) * s.units
                    residual_group(s.tile + 4 * i, HALVES[name] + 4 * i, e, i, ("ffn", layer * DT),
                                   (2 * layer + 1) * DT + 4 * i, ahead(e, 0, 1, range(2, 10 if i < 3 else 6)),
                                   2 * layer + 2 if i == 3 else None)

            def mlp(layer):
                for b, (h0, n) in enumerate(CHUNKS):
                    s, gate0 = SPANS[f"up{layer}{b}"], layer * FT + h0
                    plain, conv = PLAIN[f"up{layer}{b}"], CONV[f"up{layer}{b}"]

                    def turn(i, turns):
                        for half in range(2):
                            first = s.unit + 4 * half + 4
                            kts = ahead(first + (8 * i if turns == 1 else 0), 8, turns)
                            e = i * 8 + first
                            read_banks(i * 8 + (plain + 4 * half), i * 8 + (s.tile + 4 * half), data)
                            tails(e, 2, kts[0])
                            for k, before, done in ((1, tap0, tap1_mlp), (2, tap1_mlp, taps_done)):
                                for c in range(4):
                                    t = i * 4 + (h0 + c + half * FT)
                                    base = conv if before is tap0 else conv - mlp_conv0(layer)
                                    dve.wait_ge(before, i * 8 + (base + 4 * half + c + 1))
                                    dve.scalar_tensor_tensor(out=ACC[:, c, :], in0=back(c, k),
                                                             scalar=dcol("fconv_w", t + (layer * 3 + 2 - k) * 2 * FT),
                                                             in1=ACC[:, c, :], op0=ALU.mult, op1=ALU.add).then_inc(done, 1)
                            if half == 1:
                                for c in range(4):
                                    dve.wait_ge(silu_done, i * 4 + (gate0 + c + 1))
                                    dve.wait_ge(taps_done, i * 8 + (conv + 4 + c + 1))
                                    dve.tensor_tensor(ACC[:, c, :], ACC[:, c, :], SG[:, c, :], ALU.mult).then_inc(gated, 1)
                            tails(e, 3, kts[1])
                            if half == 1:
                                for c in range(4):
                                    dve.wait_ge(hid_head, i * 4 + (gate0 + c + 1))
                                    y = Y[:, ds(i * 4 + c, 1), :]
                                    dve.tensor_tensor(y[:, :, SEQ:2 * SEQ], ACC[:, c:c + 1, :],
                                                      y[:, :, 0:SEQ].bitcast(F32), ALU.subtract).then_inc(hid_ready, 1)
                            tails(e, 4, kts[2])
                            tails(e, 5, kts[3])

                    turns = n // 4 - (b == len(CHUNKS) - 1)
                    with dve.Fori(0, turns) as i:
                        turn(i, turns)
                    if turns < n // 4:
                        turn(turns, 1)
                    name = f"down{layer}{b}"
                    if b < len(CHUNKS) - 1:
                        residual_groups(name, 4, None, 0)
                    else:
                        gain = ("mix", DT) if layer == 0 else None
                        residual_groups(name, 2, gain, 2 * DT)
                        s = SPANS[name]
                        for i in (2, 3):
                            e = s.unit + 4 * (i + 1)
                            residual_group(s.tile + 4 * i, HALVES[name] + 4 * i, e, i, gain, 2 * DT + 4 * i, rest(e),
                                           3 if i == 3 and layer == 0 else None)

            out_projection(0)
            mlp(0)

            small_tails(2, NGATE)
            s = SPANS["in1"]
            kv_slot = {0: 8, 1: 12, 3: 16, 5: 20}
            conv, conv_base = 0, CONV["in1"]

            def rotate(c, dst):
                link(dve.tensor_tensor(SG[:, c, :], SG[:, c, :], SIN[:, :], ALU.mult))
                link(dve.tensor_tensor(ACC[:, c, :], data(c), COS[:, :], ALU.mult))
                dve.tensor_tensor(dst, ACC[:, c, :], SG[:, c, :], ALU.add).then_inc(kv_ready, 1)

            def blocks(i):
                if i:
                    dve.wait_ge(h1_done, i)
                for g in range(KVH):
                    toks = ZX[:, 8 + 4 * i + g, SEQ:2 * SEQ].rearrange("p (m r) -> p r m", r=CSTRIDE)
                    for a in range(CB // CSTRIDE):
                        l = slice(a * CSTRIDE, (a + 1) * CSTRIDE)
                        c0 = PARAMS["pe"][0] + i * CB + a * CSTRIDE
                        dve.tensor_tensor(BLK[:, l, g * NCMP:(g + 1) * NCMP], toks[:, :, a:a + NCMP],
                                          PAR[:, c0:c0 + CSTRIDE].unsqueeze(2).to_broadcast([P, CSTRIDE, NCMP]),
                                          ALU.add).then_inc(blk_ready, 1)

            def y_c_tails(q):
                dve.wait_ge(yc_head, q - 13)
                y = Y[:, 4 * (q - 14):4 * (q - 14) + 4, :]
                dve.tensor_tensor(y[:, :, SEQ:2 * SEQ], ACC[:, :, :], y[:, :, 0:SEQ].bitcast(F32), ALU.subtract)\
                   .then_inc(y_ready, 1)

            ropes = 0
            for q in range(s.groups):
                e, last = s.unit + 4 * (q + 1), q == s.groups - 1
                if q in kv_slot:
                    dst = lambda c: ZX[:, kv_slot[q] + c, SEQ:2 * SEQ]
                elif q in (10, 11):
                    dst = lambda c: CA[:, 4 * (q - 10) + c, :]
                else:
                    dst = data
                read_banks(PLAIN["in1"] + 4 * q, s.tile + 4 * q, dst)
                kts = ahead(e, 0, 1)
                if not last:
                    tails(e, 2, kts[0])
                if q in (2, 4, 6, 7, 8, 9):
                    for c in range(4):
                        ropes += 2
                        dve.wait_ge(swap_ready, ropes)
                        if q == 2:
                            rotate(c, BC[:, 2 * c, :])
                        elif q == 4:
                            rotate(c, BC[:, 2 * c + 1, :])
                        else:
                            rotate(c, ZX[:, 8 + 4 * (q - 6) + c, 0:SEQ])
                if q in (12, 13):
                    for c in range(4):
                        j = 4 * (q - 12) + c
                        dve.wait_ge(scaled, PLAIN["in1"] + 4 * q + c + 1)
                        dve.tensor_tensor(data(c), data(c), CA[:, j, :], ALU.mult).then_inc(conv_in, 1)
                    for k, before, done in ((1, tap0, tap1), (2, tap1, taps_done)):
                        for c in range(4):
                            j = 4 * (q - 12) + c
                            dve.wait_ge(before, (conv_base if k == 1 else 4 * EVEN_XBC_GROUPS) + j + 1)
                            dve.scalar_tensor_tensor(out=ACC[:, c, :] if k == 1 else CA[:, j, :], in0=back(c, k),
                                                     scalar=col("sc_w", (2 - k) * 8 + j), in1=ACC[:, c, :],
                                                     op0=ALU.mult, op1=ALU.add).then_inc(done, 1)
                if q in (14, 15):
                    for c in range(4):
                        j = 4 * (q - 14) + c
                        dve.wait_ge(taps_done, conv_base + j + 1)
                        dve.wait_ge(scaled, PLAIN["in1"] + 4 * q + c + 1)
                        dve.tensor_tensor(ACC[:, c, :], data(c), CA[:, j, :], ALU.mult).then_inc(yc_ready, 1)
                if not last:
                    tails(e, 3, kts[1])
                if q == 14:
                    y_c_tails(q)
                if q == 2:
                    small_scaled(2, NGATE, GT)
                    dve.tensor_copy(RTOK, RTOK).then_inc(gates_in, 1)
                if q == COMPRESS[0] - 1:
                    blocks(0)
                if q == COMPRESS[0] + 1:
                    blocks(1)
                if q == COMPRESS[1] + 1:
                    dve.wait_ge(kc_ready, 3)

                    def at_ends(table):
                        return table[:, CB - 1:SEQ:CSTRIDE].unsqueeze(1).to_broadcast([P, KVH, NCMP])

                    def by_head(a):
                        return a.rearrange("p (g n) -> p g n", g=KVH)

                    link(dve.tensor_tensor(by_head(KSW), by_head(KSW), at_ends(SIN), ALU.mult))
                    link(dve.tensor_tensor(by_head(KCR), by_head(KC0), at_ends(COS), ALU.mult))
                    link(dve.tensor_tensor(KCR, KCR, KSW, ALU.add))
                    dve.tensor_copy(KC0, KC0).then_inc(kv_ready, 1)
                if not last:
                    tails(e, 4, kts[2])
                    tails(e, 5, kts[3])

            dve.wait_ge(gates_ready, 1)
            dve.wait_ge(mask_ready, 1)
            items = NSA_HEADS * NT

            def branches(a, nk):
                return a.rearrange("p (r k) -> p r k", r=2)[:, :, 0:nk]

            for n in range(items + 5):
                if n in (6, 10):
                    tails(e, n // 4 + 1, kts[n // 4 - 1])
                if n < items:
                    b, t = n % 2, n % NT
                    nk = P * (t + 1)
                    p3 = PROB[:, n % 3, :]
                    if n >= 3:
                        dve.wait_ge(pt_done, n - 2)
                    dve.wait_ge(s_done, n + 1)
                    dve.tensor_tensor(p3[:, 512:512 + NCMP], bank[2 + b][:, 0:NCMP], CMPM[:, t, :], ALU.add)
                    dve.tensor_tensor(branches(p3[:, 0:512], nk), branches(bank[b][:, :], nk),
                                      MASK[:, 2 * P - nk:2 * P].unsqueeze(1).to_broadcast([P, 2, nk]), ALU.add)\
                       .then_inc(s_read, 1)
                    dve.wait_ge(s_read, n + 1)
                    dve.tensor_reduce(MX[:, 4 * b:4 * b + 1], p3[:, 512:512 + NCMP], AXX, ALU.max)
                    link(dve.tensor_reduce(MX[:, 4 * b + 1:4 * b + 3], branches(p3[:, 0:512], nk), AXX, ALU.max))
                    dve.tensor_scalar(MX[:, 4 * b:4 * b + 3], MX[:, 4 * b:4 * b + 3], -SCALE, -NEG * 1e-6,
                                      ALU.mult, ALU.min).then_inc(mx_ready, 1)
                if 1 <= n <= items:
                    m = n - 1
                    b, (h, t) = m % 2, divmod(m, NT)
                    nk = P * (t + 1)
                    dve.wait_ge(p_ready, 3 * (m + 1))
                    f = FAC[:, 4 * b:4 * b + 3]
                    if t == 0:
                        link(dve.tensor_scalar(SUMS[:, 4 * b:4 * b + 1], SUMS[:, 4 * b:4 * b + 1], 0.5, None, ALU.max))
                    link(dve.reciprocal(f, SUMS[:, 4 * b:4 * b + 3]))
                    link(dve.tensor_tensor(f, f, GT[:, t * NGATE + 3 * h:t * NGATE + 3 * h + 3], ALU.mult))
                    for r in range(2):
                        pr = PROB[:, m % 3, r * SEQ:r * SEQ + nk]
                        dve.tensor_scalar(pr, pr, FAC[:, 4 * b + 1 + r:4 * b + 2 + r], None, ALU.mult).then_inc(pn_ready, 1)
                    pr = PROB[:, m % 3, 512:512 + NCMP]
                    dve.scalar_tensor_tensor(out=pr, in0=pr, scalar=FAC[:, 4 * b:4 * b + 1], in1=CMP1[:, t, :],
                                             op0=ALU.mult, op1=ALU.mult).then_inc(pn_ready, 1)
                if n == 3:
                    y_c_tails(q)
                if n >= 6 and n % NT == 0:
                    h = n // NT - 3
                    dve.wait_ge(o_head, h + 1)
                    y = Y[:, 8 + h, :]
                    dve.tensor_tensor(y[:, SEQ:2 * SEQ], bank[6 + h % 2][:, 0:SEQ], y[:, 0:SEQ].bitcast(F32),
                                      ALU.subtract).then_inc(y_ready, 1)
            e = SPANS["out1"].unit
            for k in range(4, 10):
                tails(e, k, kt_at(e + k))
            out_projection(1)
            mlp(1)

            dve.wait_ge(stat_summed, 5)
            dve.tensor_scalar(RVAR, bank[0][:, 0:NT], 1.0 / D, EPS, ALU.mult, ALU.add).then_inc(var_ready, 1)
            dve.wait_ge(root_ready, 5)
            newton(RVAR, RSQ, RNEW, RTOK).then_inc(rstd_ready, 1)
            dve.wait_ge(rstd_ready, 5)
            for k in range(0, 4 * NT, 2):
                dve.wait_ge(out_turned, k + 1)
                dve.tensor_scalar(OST[:, k // 4, (k % 4) * 512:(k % 4 + 1) * 512], bank[4 + k % 4][:, :],
                                  RTOK[:, k // 4:k // 4 + 1], None, ALU.mult).then_inc(out_read, 1)

        @block.tensor
        def _(pe):
            def product_group(unit, tile, s, rhs, ready=None, first=False, after=None, after_unit=1):
                for u in range(s.units):
                    pe.wait_ge(tails_ready, unit + (u + 1))
                    if ready is not None:
                        pe.wait_ge(ready[0], ready[1](u) if callable(ready[1]) else
                                   ready[1] + (u + 1) * s.kt if ready[2] else ready[1])
                    for c in range(4):
                        if u == 0 and not first:
                            pe.wait_ge(bank_read, tile + (c - 3))
                        for k in range(s.kt):
                            cols = slice(k * CW + c * P, k * CW + (c + 1) * P)
                            head, tail = WHEAD[:, u % RING, cols], WTAIL[:, u % RING, cols]
                            both, one = rhs[:, u * s.kt + k, :], rhs[:, u * s.kt + k, 0:SEQ]
                            begin, end = u == 0 and k == 0, u == s.units - 1 and k == s.kt - 1
                            if begin:
                                pe.matmul(bank[c][:, :], head, both, start=True, stop=False)
                                mm = pe.matmul(bank[c][:, 0:SEQ], tail, one, start=False, stop=False)
                            else:
                                pe.matmul(bank[c][:, 0:SEQ], tail, one, start=False, stop=False)
                                mm = pe.matmul(bank[c][:, :], head, both, start=False, stop=end)
                        mm.then_inc(cols_done, 1)
                    if after and u == after_unit:
                        after()

            def product(name, rhs, ready=None, begin=0, end=None, after=None, after_unit=1):
                s = SPANS[name]
                end = s.groups if end is None else end
                if begin == 0:
                    product_group(s.unit, s.tile, s, rhs, ready, first=s.tile == 0, after=after,
                                  after_unit=after_unit)
                    begin = 1
                if end > begin:
                    with pe.Fori(begin, end) as i:
                        product_group(i * s.units + s.unit, i * 4 + s.tile, s, rhs)

            def sum_statistics(n):
                def go():
                    pe.wait_ge(stat_added, DT * n)
                    pe.matmul(bank[4][:, 0:SEQ], ONES[:, :], STAT[:, :], start=True, stop=True).then_inc(stat_summed, 1)
                return go

            def small_product(count, n):
                pe.wait_ge(ws_ready, count)
                pe.wait_ge(var_ready, 2 * count - 1)
                for t in range(NT):
                    for k in range(DT):
                        uh = U[:, k, t * P:(t + 1) * P]
                        ut = U[:, k, SEQ + t * P:SEQ + (t + 1) * P]
                        dst = bank[4][:, 64 * t:64 * t + n]
                        pe.matmul(dst, ut, WS_HEAD[:, k, 0:n], start=k == 0, stop=False)
                        pe.matmul(dst, uh, WS_TAIL[:, k, 0:n], start=False, stop=False)
                        pe.matmul(dst, uh, WS_HEAD[:, k, 0:n], start=False, stop=k == DT - 1)
                pe.wait_ge(rstd_ready, 2 * count - 1)
                for t in range(NT):
                    tr = pe.transpose(bank[5][:, t * P:(t + 1) * P], RSTD[:, t * P:(t + 1) * P], IDENT[:, :])
                tr.then_inc(rtok_turned, 1)

            pe.wait_ge(consts, CONSTS)
            pe.wait_ge(x_landed, 16 * NT)
            for k in range(8):
                if k == 2:
                    pe.wait_ge(par_first, 16 * PAR_FIRST)
                    pe.transpose(bank[0][:, 0:P], PST[:, 0, :], IDENT[:, :]).then_inc(pturned, 1)
                if k >= 4:
                    pe.wait_ge(turned_read, k - 3)
                for j in range(2):
                    for t in range(NT):
                        tr = pe.transpose(bank[4 + k % 4][:, (2 * j + t) * P:(2 * j + t + 1) * P],
                                          XST[:, t, (2 * k + j) * P:(2 * k + j + 1) * P], IDENT[:, :])
                tr.then_inc(turned, 1)
            pe.wait_ge(pturned_read, 1)
            pe.wait_ge(turned_read, 8)

            product("in0", U, (u_ready, 0, True), 0, 1, after=sum_statistics(1))
            pe.wait_ge(par_landed, 16 * (PAR_LOADS - PAR_FIRST))
            for b in range(PBANKS):
                for tile in range(4 * b + 1, min(4 * b + 5, PTILES)):
                    r = min(P, NPARAM - tile * P)
                    tr = pe.transpose(bank[5 + b][:, (tile - 1) % 4 * P:(tile - 1) % 4 * P + r], PST[0:r, tile, :],
                                      IDENT[0:r, 0:r])
                tr.then_inc(pturned, 1)
            product("in0", U, None, 1, 2)
            pe.wait_ge(pturned_read, 1 + PBANKS)
            small_product(1, HEADS)
            product("in0", U, None, 2, 5)
            pe.wait_ge(la_ready, NT)
            pe.matmul(bank[6][:, 0:HEADS], UST[:, :], LA[:, 0:HEADS], start=True, stop=True).then_inc(dte_sum, 1)
            product("in0", U, None, 5, 11)
            pe.wait_ge(x_ready, 8)
            for g in range(GROUPS):
                tr = pe.transpose(bank[7][:, g * P:(g + 1) * P], BC[:, g, 0:P], IDENT[:, :])
            tr.then_inc(bt_turned, 1)
            product("in0", U, None, 11, 12)
            pe.wait_ge(conf_dve, (CONF_TILES - POOL_CONF) * (CONF_TAPS - 1))
            pe.wait_ge(conf_pool, POOL_CONF)
            for j in range(CONF_TILES):
                mm = pe.matmul(bank[4][:, 0:SEQ], ONES[:, :], CA[:, j, :], start=j == 0, stop=j == CONF_TILES - 1)
            mm.then_inc(ln_sum, 1)
            product("in0", U, None, 12, 13)
            pe.wait_ge(ln_sq, 1)
            for j in range(CONF_TILES):
                mm = pe.matmul(bank[5][:, 0:SEQ], ONES[:, :], CP[:, j, 0:SEQ], start=j == 0, stop=j == CONF_TILES - 1)
            mm.then_inc(ln_sum, 1)
            product("in0", U, None, 13)

            pe.wait_ge(x_ready, 24)
            pe.wait_ge(btok_ready, 1)
            pe.wait_ge(ln_var, 1)
            for k in range(2 * GROUPS):
                g, t = divmod(k, 2)
                if k >= 4:
                    pe.wait_ge(xdt_ready, k - 3)
                for j in range(4):
                    tr = pe.transpose(bank[4 + k % 4][:, j * P:(j + 1) * P],
                                      ZX[:, 4 * g + j, SEQ + t * P:SEQ + (t + 1) * P], IDENT[:, :])
                tr.then_inc(xt_turned, 1)
            pe.wait_ge(bank_read, SPANS["in0"].tile_end)

            def decays(m):
                g, t = divmod(m, 2)
                pe.wait_ge(lat_ready, m + 1)
                if m == 0:
                    pe.wait_ge(xdt_ready, 2 * GROUPS)
                else:
                    pe.wait_ge(dec_ready, EXPS[m - 1])
                for h in range(2):
                    mm = pe.matmul(bank[4 + h][:, :], UST[:, :], LATS[t][:, h * 512:(h + 1) * 512], start=True, stop=True)
                mm.then_inc(d_done, 1)
                if m == 0:
                    pe.wait_ge(btok_ready, 1)
                else:
                    pe.wait_ge(cbm_ready, m)
                if m in (5, 7):
                    pe.wait_ge(ynorm_var, m // 2 - 1)
                c = slice(t * P, (t + 1) * P)
                pe.matmul(bank[2][:, 0:P], BC[:, g, c], BC[:, 4 + g, c], start=True, stop=True).then_inc(cb_done, 1)
                if t == 0:
                    pe.wait_ge(xd2_ready, g + 1)
                    pe.matmul(bank[3][:, :], BTOK[:, g, :], XD2[:, :], start=True, stop=True).then_inc(st_done, 1)
                else:
                    for h in range(2):
                        mm = pe.matmul(bank[h][:, :], ONES[:, :], LATS[t][:, h * 512:(h + 1) * 512], start=True, stop=True)
                    mm.then_inc(e_done, 1)

            def group_sum(g, dst, masked):
                pe.wait_ge(ysq_ready, g + 1)
                pe.wait_ge(cbm_ready, masked)
                pe.matmul(dst, ONES[:, :], ZX[:, 4 * g, 0:SEQ], start=True, stop=True).then_inc(ynorm_sum, 1)

            pe.wait_ge(dte_ready, 1)
            decays(0)
            for m in range(2 * GROUPS):
                g, t = divmod(m, 2)
                if m + 1 < 2 * GROUPS:
                    decays(m + 1)
                pe.wait_ge(m_ready, m + 1)
                if m >= 2:
                    pe.wait_ge(y_read, 4 * (m - 1))
                if t == 1:
                    pe.wait_ge(ce_ready, g + 1)
                    pe.wait_ge(st_ready, g + 1)
                for h in range(HPG):
                    rows, hc = slice(HP * (h % 2), HP * (h % 2) + HP), slice(h * P, (h + 1) * P)
                    dst = bank[6 + t][rows, (h // 2) * P:(h // 2 + 1) * P]
                    x_h = XDT[:, t, (HPG * g + h) * HP:(HPG * g + h + 1) * HP]
                    mm = pe.matmul(dst, x_h, DEC[:, m % 2, hc], start=True, stop=t == 0)
                    if t == 1:
                        mm = pe.matmul(dst, ST[:, h * HP:(h + 1) * HP], CE[:, hc], start=False, stop=True)
                mm.then_inc(ssd_y, 1)
                if m in (3, 5):
                    group_sum(m // 2 - 1, bank[2][:, SEQ:2 * SEQ], m + 2)
            group_sum(2, bank[5][:, 0:SEQ], 2 * GROUPS)
            product("out0", Y, (y_ready, lambda u: 2 + min((3 * u + 2) // 4, GROUPS - 1), True),
                    after=lambda: group_sum(3, bank[4][:, 0:SEQ], 2 * GROUPS), after_unit=0)

            def mlp(layer):
                for b, (h0, n) in enumerate(CHUNKS):
                    product(f"up{layer}{b}", U, (u_ready, (2 * layer + 1) * DT, True) if b == 0 else None,
                            after=sum_statistics(2 * layer + 2) if b == 0 else None)
                    product(f"down{layer}{b}", Y, (hid_ready, layer * FT + h0, True))

            mlp(0)
            product("in1", U, (u_ready, 2 * DT, True), 0, 1, after=sum_statistics(3))
            product("in1", U, None, 1, 2)
            small_product(2, NGATE)
            def compress(i):
                pe.wait_ge(w1_landed, 16 * (i + 1))
                pe.wait_ge(blk_ready, 8 * (i + 1))
                for l in range(CB):
                    mm = pe.matmul(bank[4][:, 0:KVH * NCMP], W1[:, l, :], BLK[:, l, :], start=l == 0, stop=l == CB - 1)
                mm.then_inc(h1_done, 1)

            product("in1", U, None, 2, COMPRESS[0] + 1)
            compress(0)
            product("in1", U, None, COMPRESS[0] + 1, COMPRESS[1] + 1)
            pe.wait_ge(w2_landed, 16)
            pe.wait_ge(s1_ready, 1)
            pe.matmul(bank[5][:, 0:KVH * NCMP], W2[:, 0:P], S1K, start=True, stop=True).then_inc(kc_done, 1)
            compress(1)
            product("in1", U, None, COMPRESS[1] + 1, COMPRESS[2] + 1)
            pe.wait_ge(s1_ready, 2)
            pe.wait_ge(kc_ready, 3)
            for g in range(KVH):
                mm = pe.matmul(bank[5][0:NCMP, g * HD:(g + 1) * HD], S1K[:, g * NCMP:(g + 1) * NCMP],
                               W2[:, P:2 * P], start=True, stop=True)
            mm.then_inc(kc_done, 1)
            product("in1", U, None, COMPRESS[2] + 1, SPANS["in1"].groups - 1)
            pe.wait_ge(vc_ready, 1)
            for k in range(4):
                for g in range(KVH):
                    tr = pe.transpose(bank[4 + k][:, g * P:(g + 1) * P],
                                      ZX[:, 16 + 4 * (k // 2) + g, SEQ + (k % 2) * P:SEQ + (k % 2 + 1) * P], IDENT[:, :])
                tr.then_inc(vt_turned, 1)
            product("in1", U, None, SPANS["in1"].groups - 1)

            pe.wait_ge(kv_ready, 4 * 6 + 1)
            pe.wait_ge(bank_read, SPANS["in1"].tile_end)
            items = NSA_HEADS * NT
            for n in range(items + 3):
                if n < items:
                    b, (h, t) = n % 2, divmod(n, NT)
                    g = h // (NSA_HEADS // KVH)
                    if n >= 2:
                        pe.wait_ge(s_read, n - 1)
                    if n >= 3:
                        pe.wait_ge(pt_read, 2 * (n - 2))
                    qh = ZX[:, 8 + h, t * P:(t + 1) * P]
                    if t == NT - 1:
                        pe.matmul(bank[b][:, :], qh, BC[:, 2 * g:2 * g + 2, :], start=True, stop=True)
                    else:
                        for r in range(2):
                            pe.matmul(bank[b][:, r * SEQ:r * SEQ + P], qh, BC[:, 2 * g + r, 0:P], start=True, stop=True)
                    pe.matmul(bank[2 + b][:, 0:NCMP], qh, KCR[:, g * NCMP:(g + 1) * NCMP], start=True, stop=True)\
                      .then_inc(s_done, 1)
                if 2 <= n < items + 2:
                    m = n - 2
                    b, t = m % 2, m % NT
                    pe.wait_ge(pn_ready, 3 * (m + 1))
                    pe.wait_ge(s_read, min(m + 2, items))
                    if m == 0:
                        pe.wait_ge(vt_ready, 4)
                    if m >= 2:
                        pe.wait_ge(pt_read, 2 * (m - 1))
                    i = 0
                    for r in range(2):
                        for kb in range(t + 1):
                            pe.transpose(bank[4 + b][:, i * P:(i + 1) * P],
                                         PROB[:, m % 3, r * SEQ + kb * P:r * SEQ + (kb + 1) * P], IDENT[:, :])
                            i += 1
                    pe.transpose(bank[3 - b][0:NCMP, P:2 * P], PROB[:, m % 3, 512:512 + NCMP], IDENT[:, :]).then_inc(pt_done, 1)
                if n >= 3:
                    m = n - 3
                    b, (h, t) = m % 2, divmod(m, NT)
                    g = h // (NSA_HEADS // KVH)
                    o_t = bank[6 + h % 2][:, t * P:(t + 1) * P]
                    pe.wait_ge(pt_read, 2 * (m + 1))
                    if h >= 2 and t == 0:
                        pe.wait_ge(y_ready, 5 + 2 + h - 1)
                    i = 0
                    for r in range(2):
                        for kb in range(t + 1):
                            pe.matmul(o_t, VTOK[:, kb, 4 * r + g, :], PT[:, b, i * P:(i + 1) * P],
                                      start=i == 0, stop=False)
                            i += 1
                    pe.matmul(o_t, VCT[:, g * HD:(g + 1) * HD], PTC[0:NCMP, b, :], start=False, stop=True)\
                      .then_inc(o_done, 1)
            product("out1", Y, (y_ready, 5 + 2 + NSA_HEADS, False))
            mlp(1)
            for k in range(4 * NT):
                t, b = divmod(k, 4)
                if k == 3:
                    pe.wait_ge(stat_added, 5 * DT - LAST_SQUARES)
                    pe.wait_ge(last_squared, LAST_SQUARES)
                    pe.wait_ge(bank_read, SPANS["down12"].tile_end)
                    squares = [STAT[:, :]] + [TMP[:, 4 + c - LAST_SQUARES, :] for c in range(LAST_SQUARES)]
                    for chunk in range(NT):
                        for c, sq in enumerate(squares):
                            mm = pe.matmul(bank[0][:, chunk:chunk + 1], sq[:, chunk * P:(chunk + 1) * P], ONES[:, 0:1],
                                           start=c == 0, stop=c == LAST_SQUARES)
                    mm.then_inc(stat_summed, 1)
                pe.wait_ge(out_gained, 4 * (b + 1) if t == 0 else DT)
                if k >= 4:
                    pe.wait_ge(out_read if k % 2 == 0 else store_ready, (k - 4) // 2 + 1)
                for i in range(4):
                    tr = pe.transpose(bank[4 + k % 4][:, i * P:(i + 1) * P], HG[:, 4 * b + i, t * P:(t + 1) * P], IDENT[:, :])
                tr.then_inc(out_turned, 1)


_INS = ["x", "positions", "inv_freq", "mix_norm", "ffn_norm", "final_norm", "ab_w_in", "ssm_conv_w", "ssm_conv_b",
        "ssm_dt_bias", "ssm_a_log", "ssm_d", "ssm_norm", "conf_dw_w", "conf_dw_b", "conf_ln_g", "conf_ln_b",
        "ab_w_out", "cd_w_in", "sc_conv_w", "nsa_cmp_pe", "nsa_cmp_w1", "nsa_cmp_w2", "cd_w_out",
        "ffn_w_up", "ffn_conv_w", "ffn_conv_b", "ffn_w_down"]


def kernel(**inputs):
    import numpy as _np
    import concourse.bacc as _bacc
    from concourse import mybir as _mybir
    from concourse.bass_utils import run_bass_kernel_spmd as _run

    nc = _bacc.Bacc("TRN2", target_bir_lowering=False, num_devices=1)
    half = HD // 2
    inv = _np.float32(10000.0) ** (-_np.arange(half, dtype=_np.float32) / _np.float32(half))
    constants = {"inv_freq": _np.tile(inv.astype(_np.float32), 2).reshape(P, 1)}
    arrays, args = {}, []
    for name in _INS:
        a = _np.ascontiguousarray(constants[name] if name in constants else inputs[name])
        arrays[f"in_{name}"] = a
        args.append(nc.dram_tensor(f"in_{name}", a.shape, _mybir.dt.from_np(a.dtype), kind="ExternalInput").ap())
    args.append(nc.dram_tensor("out_0", (1, SEQ, D), F32, kind="ExternalOutput").ap())
    build(nc, *args)
    r = _run(nc, [arrays], core_ids=[0])
    return r.results[0]["out_0"]
```
